# Optimizing a Trainium2 kernel written in Bass

```python
import jax, jax.numpy as jnp
from jax import lax
import numpy as np

D_MODEL = 2048
BATCH = 1
SEQ = 256
DEPTH = 1

N_MEM = 256
D_MIX = D_MODEL
ATTN_WIDTH = D_MIX // 2
SGU_WIDTH = D_MIX - ATTN_WIDTH
ATTN_HEAD_DIM = 64
N_ATTN_HEADS = ATTN_WIDTH // ATTN_HEAD_DIM
DILATED_BRANCHES = ((128, 1), (512, 4), (2048, 16))
BLOCK = 128
SGU_CHUNK = 128
SGU_GROUP_DIM = 128
N_SGU_GROUPS = SGU_WIDTH // SGU_GROUP_DIM
N_MEM_HEADS = 4
MEM_HEAD_DIM = D_MODEL // N_MEM_HEADS
D_FF = ((8 * D_MODEL // 3 + 255) // 256) * 256
D_IN = 3 * ATTN_WIDTH + 2 * SGU_WIDTH
ROPE_THETA = 10000.0
EPS = 1e-6
FFN_RES_SCALE = 0.5

kernel_name = "hybrid_dilated_attn_sgu_macaron_layer"

def _rmsnorm(x, g):
    x32 = x.astype(jnp.float32)
    y = x32 * lax.rsqrt(jnp.mean(x32 * x32, axis=-1, keepdims=True) + EPS)
    return (y * g.astype(jnp.float32)).astype(x.dtype)

def _layernorm(x, g, b):
    x32 = x.astype(jnp.float32)
    mu = jnp.mean(x32, axis=-1, keepdims=True)
    xc = x32 - mu
    y = xc * lax.rsqrt(jnp.mean(xc * xc, axis=-1, keepdims=True) + EPS)
    return (y * g.astype(jnp.float32) + b.astype(jnp.float32)).astype(x.dtype)

def _swiglu(x, w_gate, w_up, w_down):
    return (jax.nn.silu(x @ w_gate) * (x @ w_up)) @ w_down

def _rope(t, positions):
    e = t.shape[-1]
    inv_freq = ROPE_THETA ** (-jnp.arange(0, e, 2, dtype=jnp.float32) / e)
    ang = positions.astype(jnp.float32)[..., None] * inv_freq
    cos = jnp.cos(ang)[:, :, None, :]
    sin = jnp.sin(ang)[:, :, None, :]
    t32 = t.astype(jnp.float32)
    t1, t2 = t32[..., : e // 2], t32[..., e // 2:]
    return jnp.concatenate([t1 * cos - t2 * sin, t1 * sin + t2 * cos], axis=-1).astype(t.dtype)

def _dilated_branch(q, k, v, window, dilation):
    b, s, h, e = q.shape
    steps = window // dilation
    sub_len = s // dilation
    n_blk = -(-sub_len // BLOCK)
    pad = n_blk * BLOCK - sub_len

    def split(t):
        return t.reshape(b, sub_len, dilation, h, e).transpose(0, 2, 1, 3, 4)

    qs = jnp.pad(split(q), ((0, 0), (0, 0), (0, pad), (0, 0), (0, 0)))
    kv_pad = ((0, 0), (0, 0), (BLOCK, pad), (0, 0), (0, 0))
    ks = jnp.pad(split(k), kv_pad).reshape(b, dilation, n_blk + 1, BLOCK, h, e)
    vs = jnp.pad(split(v), kv_pad).reshape(b, dilation, n_blk + 1, BLOCK, h, e)
    qb = qs.reshape(b, dilation, n_blk, BLOCK, h, e)
    kb = jnp.concatenate([ks[:, :, :-1], ks[:, :, 1:]], axis=3)
    vb = jnp.concatenate([vs[:, :, :-1], vs[:, :, 1:]], axis=3)

    scores = jnp.einsum('brnqhe,brnkhe->brnhqk', qb, kb).astype(jnp.float32) * (e ** -0.5)
    qi = jnp.arange(BLOCK)[:, None]
    kj = jnp.arange(2 * BLOCK)[None, :]
    diff = qi + BLOCK - kj
    band = (diff >= 0) & (diff <= steps)
    blk = jnp.arange(n_blk)[:, None, None]
    valid = band[None] & ((blk > 0) | (kj[None] >= BLOCK))
    scores = jnp.where(valid[None, None, :, None], scores, -jnp.inf)
    m = jnp.max(scores, axis=-1, keepdims=True)
    p = jnp.exp(scores - m)
    l = jnp.sum(p, axis=-1, keepdims=True)
    o = jnp.einsum('brnhqk,brnkhe->brnqhe', (p / l).astype(v.dtype), vb)
    lse = (m + jnp.log(l))[..., 0]

    o = o.reshape(b, dilation, n_blk * BLOCK, h, e)[:, :, :sub_len]
    o = o.transpose(0, 2, 1, 3, 4).reshape(b, s, h, e)
    lse = lse.transpose(0, 1, 2, 4, 3).reshape(b, dilation, n_blk * BLOCK, h)[:, :, :sub_len]
    lse = lse.transpose(0, 2, 1, 3).reshape(b, s, h)
    return o, lse

def _dilated_attention(q, k, v):
    outs, lses = [], []
    for window, dilation in DILATED_BRANCHES:
        o, lse = _dilated_branch(q, k, v, window, dilation)
        outs.append(o)
        lses.append(lse)
    wts = jax.nn.softmax(jnp.stack(lses, axis=0), axis=0)
    return jnp.einsum('nbsh,nbshe->bshe', wts.astype(v.dtype), jnp.stack(outs, axis=0))

def _spatial_gating(u, gv, ln_g, ln_b, w_s, b_s):
    b, s, _ = gv.shape
    u = jax.nn.gelu(u)
    gv = _layernorm(jax.nn.gelu(gv), ln_g, ln_b)
    nc = s // SGU_CHUNK
    vc = gv.reshape(b, nc, SGU_CHUNK, N_SGU_GROUPS, SGU_GROUP_DIM)
    causal = jnp.tril(jnp.ones((SGU_CHUNK, SGU_CHUNK), dtype=bool))
    w = jnp.where(causal[None], w_s, 0.0).astype(gv.dtype)
    sv = jnp.einsum('gij,bcjgd->bcigd', w, vc) + b_s.T.astype(gv.dtype)[None, None, :, :, None]
    return u * sv.reshape(b, s, SGU_WIDTH)

def _token_mixing(h, positions, norm_g, w_in, ln_g, ln_b, w_s, b_s, attn_g, sgu_g, w_out):
    b, s, _ = h.shape
    xn = _rmsnorm(h, norm_g)
    proj = xn @ w_in
    q, k, v, u, gv = jnp.split(
        proj, [ATTN_WIDTH, 2 * ATTN_WIDTH, 3 * ATTN_WIDTH, 3 * ATTN_WIDTH + SGU_WIDTH], axis=-1)
    q = _rope(q.reshape(b, s, N_ATTN_HEADS, ATTN_HEAD_DIM), positions)
    k = _rope(k.reshape(b, s, N_ATTN_HEADS, ATTN_HEAD_DIM), positions)
    v = v.reshape(b, s, N_ATTN_HEADS, ATTN_HEAD_DIM)
    attn = _dilated_attention(q, k, v).reshape(b, s, ATTN_WIDTH)
    sgu = _spatial_gating(u, gv, ln_g, ln_b, w_s, b_s)
    mixed = jnp.concatenate([_rmsnorm(attn, attn_g), _rmsnorm(sgu, sgu_g)], axis=-1)
    return mixed @ w_out

def _memory_cross_attention(h, mem, g_q, g_kv, w_q, w_k, w_v, w_o):
    b, s, _ = h.shape
    n_mem = mem.shape[1]
    xq = _rmsnorm(h, g_q)
    mk = _rmsnorm(mem, g_kv)
    q = (xq @ w_q).reshape(b, s, N_MEM_HEADS, MEM_HEAD_DIM)
    k = (mk @ w_k).reshape(b, n_mem, N_MEM_HEADS, MEM_HEAD_DIM)
    v = (mk @ w_v).reshape(b, n_mem, N_MEM_HEADS, MEM_HEAD_DIM)
    scores = jnp.einsum('bshe,bmhe->bhsm', q, k).astype(jnp.float32) * (MEM_HEAD_DIM ** -0.5)
    p = jax.nn.softmax(scores, axis=-1).astype(v.dtype)
    o = jnp.einsum('bhsm,bmhe->bshe', p, v).reshape(b, s, D_MODEL)
    return o @ w_o

def setup_inputs(seed: int = 0) -> dict:
    key = jax.random.key(seed)
    ks = jax.random.split(key, 32)
    f32 = jnp.float32
    L = DEPTH

    def w(k, shape, fan_in):
        return jax.random.normal(k, shape, f32) * fan_in ** -0.5

    def gain(k, shape):
        return 1.0 + 0.01 * jax.random.normal(k, shape, f32)

    return {
        "x": jax.random.normal(ks[0], (BATCH, SEQ, D_MODEL), f32),
        "mem": jax.random.normal(ks[1], (BATCH, N_MEM, D_MODEL), f32),
        "positions": jnp.broadcast_to(jnp.arange(SEQ, dtype=jnp.int32), (BATCH, SEQ)),
        "ffn1_norm": gain(ks[2], (L, D_MODEL)),
        "ffn1_w_gate": w(ks[3], (L, D_MODEL, D_FF), D_MODEL),
        "ffn1_w_up": w(ks[4], (L, D_MODEL, D_FF), D_MODEL),
        "ffn1_w_down": w(ks[5], (L, D_FF, D_MODEL), D_FF),
        "mix_norm": gain(ks[6], (L, D_MODEL)),
        "w_in": w(ks[7], (L, D_MODEL, D_IN), D_MODEL),
        "sgu_ln_gain": gain(ks[8], (L, SGU_WIDTH)),
        "sgu_ln_bias": 0.01 * jax.random.normal(ks[9], (L, SGU_WIDTH), f32),
        "sgu_w_s": w(ks[10], (L, N_SGU_GROUPS, SGU_CHUNK, SGU_CHUNK), SGU_CHUNK),
        "sgu_b_s": 1.0 + 0.1 * jax.random.normal(ks[11], (L, N_SGU_GROUPS, SGU_CHUNK), f32),
        "attn_out_gain": gain(ks[12], (L, ATTN_WIDTH)),
        "sgu_out_gain": gain(ks[13], (L, SGU_WIDTH)),
        "w_out": w(ks[14], (L, D_MIX, D_MODEL), D_MIX),
        "mem_q_norm": gain(ks[15], (L, D_MODEL)),
        "mem_kv_norm": gain(ks[16], (L, D_MODEL)),
        "mem_w_q": w(ks[17], (L, D_MODEL, D_MODEL), D_MODEL),
        "mem_w_k": w(ks[18], (L, D_MODEL, D_MODEL), D_MODEL),
        "mem_w_v": w(ks[19], (L, D_MODEL, D_MODEL), D_MODEL),
        "mem_w_o": w(ks[20], (L, D_MODEL, D_MODEL), D_MODEL),
        "ffn2_norm": gain(ks[21], (L, D_MODEL)),
        "ffn2_w_gate": w(ks[22], (L, D_MODEL, D_FF), D_MODEL),
        "ffn2_w_up": w(ks[23], (L, D_MODEL, D_FF), D_MODEL),
        "ffn2_w_down": w(ks[24], (L, D_FF, D_MODEL), D_FF),
        "final_norm": gain(ks[25], (D_MODEL,)),
    }

def reference(x, mem, positions,
              ffn1_norm, ffn1_w_gate, ffn1_w_up, ffn1_w_down,
              mix_norm, w_in, sgu_ln_gain, sgu_ln_bias, sgu_w_s, sgu_b_s,
              attn_out_gain, sgu_out_gain, w_out,
              mem_q_norm, mem_kv_norm, mem_w_q, mem_w_k, mem_w_v, mem_w_o,
              ffn2_norm, ffn2_w_gate, ffn2_w_up, ffn2_w_down,
              final_norm):
    h = x
    for layer in range(DEPTH):
        h = h + FFN_RES_SCALE * _swiglu(_rmsnorm(h, ffn1_norm[layer]),
                                        ffn1_w_gate[layer], ffn1_w_up[layer], ffn1_w_down[layer])
        h = h + _token_mixing(h, positions, mix_norm[layer], w_in[layer],
                              sgu_ln_gain[layer], sgu_ln_bias[layer], sgu_w_s[layer], sgu_b_s[layer],
                              attn_out_gain[layer], sgu_out_gain[layer], w_out[layer])
        h = h + _memory_cross_attention(h, mem, mem_q_norm[layer], mem_kv_norm[layer],
                                        mem_w_q[layer], mem_w_k[layer], mem_w_v[layer], mem_w_o[layer])
        h = h + FFN_RES_SCALE * _swiglu(_rmsnorm(h, ffn2_norm[layer]),
                                        ffn2_w_gate[layer], ffn2_w_up[layer], ffn2_w_down[layer])
    return _rmsnorm(h, final_norm)


_drawn_inputs = setup_inputs


def setup_inputs(seed=0):
    import zlib

    import numpy as np

    out = dict(_drawn_inputs(seed))
    spreads = {}
    factors = {'ffn1_norm': 8.0,
     'mix_norm': 5.437,
     'sgu_ln_gain': 200.0,
     'sgu_ln_bias': 200.0,
     'attn_out_gain': 200.0,
     'sgu_out_gain': 200.0,
     'mem_q_norm': 32.953,
     'mem_kv_norm': 33.945,
     'ffn2_norm': 181.828,
     'final_norm': 161.721,
     'sgu_b_s': 14.393}
    for name, (base, spread) in spreads.items():
        noise = np.random.default_rng([zlib.crc32(name.encode()), seed]).standard_normal(out[name].shape)
        drawn = base * np.exp(spread * noise) if base else spread * noise
        out[name] = __import__('jax').numpy.asarray(drawn.astype(out[name].dtype))
    for name, factor in factors.items():
        out[name] = (out[name] * factor).astype(out[name].dtype)
    return out
```

```python
from contextlib import ExitStack

import numpy as np

import concourse.bass as bass
from concourse import mybir

ALU = mybir.AluOpType
ACT = mybir.ActivationFunctionType
F32 = mybir.dt.float32
F32R = mybir.dt.float32r
I32 = mybir.dt.int32
AX_X = mybir.AxisListType.X

P = 128
D = 2048
S = 256
TT = S // P
FF = 5632
NC = 512
KT = D // P
AW = 1024
NH, HD = 16, 64
NG = 8
MH, MHD = 4, 512
EPS = 1e-6
THETA = 10000.0
ATT_SCALE = HD ** -0.5
MEM_SCALE = MHD ** -0.5
NEG = -1e30

RAW = 4
RING = 4
AHEAD = 4
FCH = FF // NC

FFN_HALVES = FCH * 24
M_F1 = 0
M_WIN = M_F1 + FFN_HALVES
M_MKV = M_WIN + 80
M_WO = M_MKV + 64
M_MQ = M_WO + 32
M_MO = M_MQ + 32
M_F2 = M_MO + 32
M_END = M_F2 + FFN_HALVES

U_F1 = 0
U_WIN = U_F1 + 2 * FCH
U_MKV = U_WIN + 5
U_WO = U_MKV + 4
U_MQ = U_WO + 2
U_MO = U_MQ + 2
U_F2 = U_MO + 2

G_FFN1, G_MIX, G_MEMQ, G_MEMKV, G_FFN2, G_ATTN, G_SGU, B_SGU = 0, 16, 32, 48, 64, 80, 88, 96
NVEC = 104

PAIRS = ("gv", "u", "q", "k", "v")
PAIR_COL = {"q": 0, "k": AW, "v": 2 * AW, "u": 3 * AW, "gv": 4 * AW}

C_ID, C_MASK, C_FREQ, C_END = 0, 128, 512, 544


def unit_numbers():
    order = [("cols",)]
    order += [("x", j) for j in range(8)]
    order += [("a1", i, j) for i in range(FCH) for j in range(2)]
    order += [("h1", j) for j in range(8)] + [("ws", 0), ("ws", 1)]
    order += [("mem", j) for j in range(8)]
    for k in range(NH + 1):
        if k:
            order.append(("p", k - 1))
        if k < NH:
            if k % 2 == 0:
                order.append(("qk", k // 2))
            if k % 2 == 0 and 2 <= k <= 8:
                order += [("mk", k // 2 - 1, 0), ("mk", k // 2 - 1, 1)]
            if k % 2 and k < 8:
                order.append(("sgu", k // 2))
    order += [("att", j) for j in range(4)]
    order += [("h2", j) for j in range(6)]
    order += [("h2", 6), ("h2", 7)]
    for c in range(MH):
        order += [("mq", c, 0), ("mq", c, 1), ("mp", c), ("o", c, 0), ("o", c, 1)]
    order += [("h3", j) for j in range(8)]
    order += [("a2", i, j) for i in range(FCH) for j in range(2)]
    number = {name: n for n, name in enumerate(order)}
    split = [n for n in order if n[0] in ("x", "a1", "h1", "mem", "sgu", "att", "h2", "o", "h3", "a2")]
    return number, {name: n for n, name in enumerate(split)}


UNIT, SPLIT = unit_numbers()


def layer_program(nc, a, out):
    with ExitStack() as ctx:
        def sb(name, shape, dt=F32):
            return ctx.enter_context(nc.sbuf_tensor(name, shape, dt))

        def sem(name):
            return ctx.enter_context(nc.semaphore(name))

        h = sb("h", [P, TT, D])
        x_hi, x_lo = sb("x_hi", [P, KT, S], F32R), sb("x_lo", [P, KT, S], F32R)
        y_hi, y_lo = sb("y_hi", [P, KT, S], F32R), sb("y_lo", [P, KT, S], F32R)
        raw = sb("raw", [P, RAW, 4, NC])
        w_hi, w_lo = sb("w_hi", [P, RING, 2, NC], F32R), sb("w_lo", [P, RING, 2, NC], F32R)
        qk = sb("qk", [P, TT, 2, AW])
        v = sb("v", [P, TT, AW])
        memv = sb("memv", [P, TT, D])
        memk_t = sb("memk_t", [P, KT, S])
        att = sb("att", [P, TT, AW])
        tmp = sb("tmp", [P, 2048])
        junk = sb("junk", [P, NC])
        const = sb("const", [P, C_END])
        cols = sb("cols", [P, NVEC])
        trig = sb("trig", [P, 2, TT, 32])
        pos = sb("pos", [P, TT], I32)
        stat = sb("stat", [P, 72])

        ident = const[:, C_ID:C_ID + P]
        aT_hi, aT_lo = y_hi[:, 12:16, :], y_lo[:, 12:16, :]
        att_flat = att[:, :, :].rearrange("p t n -> p (t n)")
        silu = att_flat[:, 0:1024].rearrange("p (t n) -> p t n", t=TT)
        hid = att_flat[:, 1024:2048].rearrange("p (t n) -> p t n", t=TT)
        rope_tmp = att_flat[:, 0:1024].rearrange("p (r n) -> p r n", r=4)
        mem_nat = memk_t[:, :, :].rearrange("p k s -> p (k s)").rearrange("p (t n) -> p t n", t=TT)
        memv_flat = memv[:, :, :].rearrange("p t n -> p (t n)")
        u = memv_flat[:, 0:2048].rearrange("p (t n) -> p t n", t=TT)
        gv = memv_flat[:, 2048:4096].rearrange("p (t n) -> p t n", t=TT)
        mk_nat = memv_flat[:, 2048:3072].rearrange("p (t n) -> p t n", t=TT)
        ln_gain, ln_bias = tmp[:, 0:1024], tmp[:, 1024:2048]
        qk_t = tmp[:, 0:512]
        sm, pr, pr_t = tmp[:, 512:896], tmp[:, 896:1280], tmp[:, 1280:1664]
        qk_flat = qk[:, :, :, :].rearrange("p t w n -> p (t w n)")
        mq_nat = qk_flat[:, 0:1024].rearrange("p (t n) -> p t n", t=TT)
        mq_t = qk_flat[:, 1024:2048].rearrange("p (k s) -> p k s", k=4)
        mp = qk_flat[:, 2048:2560].rearrange("p (t m) -> p t m", t=TT)
        mp_t = qk_flat[:, 2560:3072].rearrange("p (m q) -> p m q", m=TT)
        mo_nat = qk_flat[:, 3072:4096].rearrange("p (t n) -> p t n", t=TT)
        ws_nat = qk_flat[:, 0:1024].rearrange("p (g j) -> p g j", g=NG)
        vec_rows = qk_flat[:, 1024:1152]
        v_flat = v[:, :, :].rearrange("p t n -> p (t n)")
        ws_t = att_flat[:, 1024:2048].rearrange("p (g i) -> p g i", g=NG)
        final_gain = v_flat
        y_out = mem_nat

        ssq = stat[:, 0:8].rearrange("p (t c) -> p t c", t=TT)
        var = stat[:, 8:10]
        rstd = stat[:, 10:12]
        n0, n1, n2 = stat[:, 12:14], stat[:, 14:16], stat[:, 16:18]
        mem_ssq = stat[:, 18:26].rearrange("p (t c) -> p t c", t=TT)
        mem_rstd = stat[:, 26:28]
        gv_sum = stat[:, 28:32].rearrange("p (t c) -> p t c", t=TT)
        gv_mean = stat[:, 32:34]
        gv_ssq = stat[:, 62:66].rearrange("p (t c) -> p t c", t=TT)
        gv_rstd = stat[:, 34:36]
        sgu_ssq = stat[:, 36:40].rearrange("p (t c) -> p t c", t=TT)
        sgu_rstd = stat[:, 40:42]
        att_ssq = stat[:, 42:50].rearrange("p (t c) -> p t c", t=TT)
        att_rstd = stat[:, 50:52]
        root = stat[:, 52:54]
        s_max, s_neg = stat[:, 54:56], stat[:, 56:58]
        s_sum, s_inv = stat[:, 58:60], stat[:, 60:62]

        bank = ctx.enter_context(nc.psum_tensor("bank", [P, 8, NC], F32))

        landed = [sem(f"slab_landed_{s}") for s in range(RAW)]
        hi_ready, lo_ready = sem("hi_ready"), sem("lo_ready")
        half_used = sem("half_used")
        pair_free = [sem(f"pair_free_{p}") for p in range(3)]
        tr_done = sem("tr_done")
        tr_hi = sem("tr_hi")
        tr_free = [sem("tr_free_6"), sem("tr_free_7")]
        squared, root_ready, var_ready = sem("squared"), sem("root_ready"), sem("var_ready")
        rstd_ready = sem("rstd_ready")
        const_in, vec_in, ws_in, ln_in, mem_in, pos_in = (
            sem(n) for n in ("const_in", "vec_in", "ws_in", "ln_in", "mem_in", "pos_in"))
        x_in = [sem(f"x_in_{c}") for c in range(4)]
        ws_masked = sem("ws_masked")
        trig_arg, trig_ready = sem("trig_arg"), sem("trig_ready")
        centred, gv_ready = sem("centred"), sem("gv_ready")
        sv_done, sgu_ready, sgu_scaled = sem("sv_done"), sem("sgu_ready"), sem("sgu_scaled")
        rope_done = sem("rope_done")
        s_done, s_masked, p_ready = sem("s_done"), sem("s_masked"), sem("p_ready")
        pv_done, o_ready, att_scaled = sem("pv_done"), sem("o_ready"), sem("att_scaled")
        ms_done, mmax_ready, mp_ready = (sem(n) for n in ("ms_done", "mmax_ready", "mp_ready"))
        mpv_done, mo_ready = sem("mpv_done"), sem("mo_ready")
        gain_in, y_ready, out_done = sem("gain_in"), sem("y_ready"), sem("out_done")
        step = sem("vector_step")

        block = ctx.enter_context(nc.Block())

        def f32(ap):
            return ap.bitcast(F32)

        def pair_bank(pair, t):
            return bank[:, 2 * pair + t, :]

        def read_out(eng, pair, use, t=1):
            eng.wait_ge(pair_free[pair], 2 * use + t + 1)

        def ffn_final(uses, uses2):
            last = uses + 2 * FCH - 1
            return [(2, uses2 + 2 * FCH - 2), (0, last), (2, uses2 + 2 * FCH - 1), (1, last)]

        final = {"h1": ffn_final(U_F1, 0), "h2": [(c % 2, U_WO + c // 2) for c in range(4)],
                 "h3": [(c % 2, U_MO + c // 2) for c in range(4)], "h4": ffn_final(U_F2, 2 * FCH)}

        @block.sync
        def _(sp):
            def load(m, j, w, row, col):
                if not isinstance(m, int) or m >= 2 * RAW:
                    sp.wait_ge(lo_ready, m - 2 * RAW + 2)
                slot = (j // 2) % RAW
                src = w[bass.ds(row, 512), bass.ds(col, NC)].rearrange("(k p) n -> p k n", p=P)
                sp.dma_start(raw[:, slot, :, :], src).then_inc(landed[slot], 16)

            def ffn_loads(m0, gate, up, down):
                for w, j0 in ((gate, 0), (up, 8)):
                    for s in range(4):
                        load(m0 + j0 + 2 * s, j0 + 2 * s, w, 512 * s, 0)
                with sp.Fori(0, FCH - 1) as i:
                    row, col, m = sp.snap(i * NC), sp.snap(i * NC + NC), sp.snap(i * 24 + (m0 + 16))
                    for w, j0 in ((gate, 0), (up, 8)):
                        for s in range(4):
                            load(m + (j0 + 2 * s), j0 + 2 * s, w, 512 * s, col)
                    for c in range(4):
                        load(m + (16 + 2 * c), 2 * c, down, row, NC * c)
                for c in range(4):
                    load(m0 + FFN_HALVES - 8 + 2 * c, 2 * c, down, (FCH - 1) * NC, NC * c)

            def square_loads(m0, w):
                with sp.Fori(0, D // NC) as c:
                    col, m = sp.snap(c * NC), sp.snap(c * 8 + m0)
                    for s in range(4):
                        load(m + 2 * s, 2 * s, w, 512 * s, col)

            ffn_loads(M_F1, a["ffn1_w_gate"], a["ffn1_w_up"], a["ffn1_w_down"])
            for n, name in enumerate(PAIRS):
                for c in range(2):
                    for s in range(4):
                        j = 16 * n + 8 * c + 2 * s
                        load(M_WIN + j, j, a["w_in"], 512 * s, PAIR_COL[name] + NC * c)
            square_loads(M_MKV, a["mem_w_k"])
            square_loads(M_MKV + 32, a["mem_w_v"])
            for c in range(4):
                for s, row in enumerate((1024, 1536, 0, 512)):
                    load(M_WO + 8 * c + 2 * s, 2 * s, a["w_out"], row, NC * c)
            square_loads(M_MQ, a["mem_w_q"])
            square_loads(M_MO, a["mem_w_o"])
            ffn_loads(M_F2, a["ffn2_w_gate"], a["ffn2_w_up"], a["ffn2_w_down"])
            for t in range(TT):
                for c in range(2):
                    sp.wait_ge(y_ready, 2 * t + c + 1)
                    sp.dma_start(out[t * P:(t + 1) * P, c * AW:(c + 1) * AW],
                                 y_out[:, t, c * AW:(c + 1) * AW]).then_inc(out_done, 16)
            sp.wait_ge(out_done, 64)

        @block.gpsimd
        def _(pool):
            pool.wait_ge(ws_in, 16)
            nc.gpsimd.affine_select(out=ws_nat, in_=ws_nat, compare_op=ALU.is_ge, fill=0.0, base=0,
                                    pattern=[[0, NG], [-1, P]], channel_multiplier=1).then_inc(ws_masked, 1)

        @block.tensor
        def _(pe):
            def half(m, j, pair, kt, src_hi, src_lo, first, last):
                pe.wait_ge(lo_ready, m + 1)
                slot = j % RING
                for k in range(2):
                    for t in range(TT):
                        hi = src_hi[:, kt + k, t * P:(t + 1) * P]
                        lo = src_lo[:, kt + k, t * P:(t + 1) * P]
                        begin, end = first and k == 0, last and k == 1
                        o = pair_bank(pair, t)
                        nc.tensor.matmul(o, hi, w_hi[:, slot, k, :], start=begin, stop=False)
                        nc.tensor.matmul(o, hi, w_lo[:, slot, k, :], start=False, stop=False)
                        mm = nc.tensor.matmul(o, lo, w_hi[:, slot, k, :], start=False, stop=end)
                mm.then_inc(half_used, 1)

            def take_pair(pair, uses):
                if not isinstance(uses, int) or uses > 0:
                    pe.wait_ge(pair_free[pair], uses * 2)

            def unit_bank(n):
                if n >= 2:
                    pe.wait_ge(tr_free[n % 2], n // 2)
                return bank[:, 6 + n % 2, :]

            def transposed(n):
                pe.wait_ge(tr_free[n % 2], n // 2 + 1)

            def transpose_unit(n, src, kt):
                o = unit_bank(n)
                for k in range(2):
                    for t in range(TT):
                        tr = nc.tensor.transpose(o[:, (2 * k + t) * P:(2 * k + t + 1) * P],
                                                 src[:, t, (kt + k) * P:(kt + k + 1) * P], ident)
                tr.then_inc(tr_done, 1)

            def h_unit(name, j):
                read_out(pe, *final[name][j // 2])
                transpose_unit(UNIT[(name, j)], h, 2 * j)

            def square_chunk(m0, j0, pair, src_hi, src_lo, after, kts=(0, 2, 4, 6, 8, 10, 12, 14)):
                for j, kt in enumerate(kts):
                    half(m0 + j, j0 + j, pair, kt, src_hi, src_lo, j == 0, j == 7)
                    after(j)

            def nothing(j):
                pass

            def ffn(m0, uses, uses2, name, before_gate, after_down):
                def down(m, j0, u01, u2):
                    for c, (pair, used) in enumerate(((2, u2), (0, u01[0]), (2, u2 + 1), (1, u01[1]))):
                        take_pair(pair, used)
                        for n in range(2):
                            half(m + 2 * c + n, j0 + 2 * c + n, pair, 2 * n, aT_hi, aT_lo, n == 0, n == 1)
                        yield c

                take_pair(0, uses)
                for j in range(8):
                    before_gate(j)
                    half(m0 + j, j, 0, 2 * j, x_hi, x_lo, j == 0, j == 7)
                take_pair(1, uses)
                square_chunk(m0 + 8, 0, 1, x_hi, x_lo, nothing)
                n0_ = UNIT[(name, 0, 0)]
                with pe.Fori(0, FCH - 1) as i:
                    m = i * 24 + (m0 + 16)
                    take_pair(0, i * 2 + (uses + 1))
                    square_chunk(m, 0, 0, x_hi, x_lo, nothing)
                    take_pair(1, i * 2 + (uses + 1))
                    for n in range(2):
                        b = (n0_ + n) % 2
                        pe.wait_ge(tr_free[b], i + (n0_ + n) // 2)
                        for k in range(2):
                            for t in range(TT):
                                tr = nc.tensor.transpose(
                                    bank[:, 6 + b, (2 * k + t) * P:(2 * k + t + 1) * P],
                                    hid[:, t, (2 * n + k) * P:(2 * n + k + 1) * P], ident)
                        tr.then_inc(tr_done, 1)
                    square_chunk(m + 8, 8, 1, x_hi, x_lo, nothing)
                    for n in range(2):
                        pe.wait_ge(tr_free[(n0_ + n) % 2], i + ((n0_ + n) // 2 + 1))
                    for _ in down(m + 16, 16, (i * 2 + (uses + 2), i * 2 + (uses + 2)), i * 2 + uses2):
                        pass
                read_out(pe, 1, uses + 2 * FCH - 3)
                for n in range(2):
                    transpose_unit(UNIT[(name, FCH - 1, n)], hid, 2 * n)
                for n in range(2):
                    transposed(UNIT[(name, FCH - 1, n)])
                last = uses + 2 * FCH - 1
                for c in down(m0 + FFN_HALVES - 8, 0, (last, last), uses2 + 2 * FCH - 2):
                    after_down(c)

            pe.wait_ge(const_in, 16)
            pe.wait_ge(vec_in, 8 * 16)
            o = unit_bank(UNIT[("cols",)])
            nc.tensor.transpose(o[:, 0:NVEC], vec_rows[0:NVEC, :], ident[0:NVEC, 0:NVEC]).then_inc(tr_done, 1)

            def ws_unit(n):
                pe.wait_ge(ws_masked, 1)
                o = unit_bank(UNIT[("ws", n)])
                for g in range(4):
                    tr = nc.tensor.transpose(o[:, g * P:(g + 1) * P], ws_nat[:, 4 * n + g, :], ident)
                tr.then_inc(tr_done, 1)

            def x_unit(j):
                if j % 2 == 0:
                    pe.wait_ge(x_in[j // 2], 16)
                transpose_unit(UNIT[("x", j)], h, 2 * j)

            def x_units(j):
                if j == 0:
                    x_unit(0)
                    x_unit(1)
                if j + 2 < 8:
                    x_unit(j + 2)
                transposed(UNIT[("x", j)])

            def h1_units(c):
                if c:
                    h_unit("h1", 2 * c - 2)
                    h_unit("h1", 2 * c - 1)

            ffn(M_F1, U_F1, 0, "a1", x_units, h1_units)

            def last_h_units(name):
                def after(j):
                    if j in (1, 2):
                        h_unit(name, 5 + j)
                    if j in (3, 4) and name == "h1":
                        ws_unit(j - 3)
                    if j in (5, 6):
                        transposed(UNIT[(name, j + 1)])
                return after

            for j in range(6):
                transposed(UNIT[("h1", j)])
            take_pair(0, U_WIN)
            square_chunk(M_WIN, 0, 0, y_hi, y_lo, last_h_units("h1"))
            take_pair(1, U_WIN)
            square_chunk(M_WIN + 8, 8, 1, y_hi, y_lo, nothing)
            with pe.Fori(0, 3) as i:
                m = i * 16 + (M_WIN + 16)
                take_pair(0, i + (U_WIN + 1))
                square_chunk(m, 0, 0, y_hi, y_lo, nothing)
                take_pair(1, i + (U_WIN + 1))
                square_chunk(m + 8, 8, 1, y_hi, y_lo, nothing)

            def mem_units(j):
                if j == 0:
                    pe.wait_ge(mem_in, 16)
                transpose_unit(UNIT[("mem", j)], mem_nat, 2 * j)

            def spatial(j):
                if j % 2 or j > 6:
                    return
                t, n = j // 2 // 2, j // 2 % 2
                if j == 0:
                    transposed(UNIT[("ws", 1)])
                    pe.wait_ge(gv_ready, 2)
                    pe.wait_ge(pair_free[2], (2 * FCH) * 2)
                if t == 1:
                    pe.wait_ge(sgu_ready, 4 * n + 4)
                for g in range(4):
                    gg = 4 * n + g
                    mm = nc.tensor.matmul(bank[:, 4 + n, g * P:(g + 1) * P], ws_t[:, gg, :],
                                          gv[:, t, gg * P:(gg + 1) * P], start=True, stop=True)
                mm.then_inc(sv_done, 1)

            take_pair(0, U_WIN + 4)
            square_chunk(M_WIN + 64, 0, 0, y_hi, y_lo, mem_units)
            take_pair(1, U_WIN + 4)
            square_chunk(M_WIN + 72, 8, 1, y_hi, y_lo, spatial)

            def scores(k):
                if k % 2 == 0:
                    transposed(UNIT[("qk", k // 2)])
                if k:
                    pe.wait_ge(s_masked, k)
                else:
                    pe.wait_ge(sgu_ready, 16)
                r = HD * (k % 2)
                q, kk = qk_t[r:r + HD, 0:256], qk_t[r:r + HD, 256:512]
                nc.tensor.matmul(bank[:, 4, 0:P], q[:, 0:P], kk[:, 0:P], start=True, stop=True)
                nc.tensor.matmul(bank[:, 4, P:3 * P], q[:, P:2 * P], kk, start=True,
                                 stop=True).then_inc(s_done, 1)

            def p_unit(k):
                o = unit_bank(UNIT[("p", k)])
                pe.wait_ge(p_ready, k + 1)
                for b in range(3):
                    tr = nc.tensor.transpose(o[:, b * P:(b + 1) * P], pr[:, b * P:(b + 1) * P], ident)
                tr.then_inc(tr_done, 1)

            def weigh(k):
                transposed(UNIT[("p", k)])
                if k:
                    pe.wait_ge(o_ready, k)
                e = slice(HD * k, HD * k + HD)
                nc.tensor.matmul(bank[:, 5, 0:HD], pr_t[:, 0:P], v[:, 0, e], start=True, stop=True)
                nc.tensor.matmul(bank[:, 5, HD:2 * HD], pr_t[:, P:2 * P], v[:, 0, e], start=True, stop=False)
                nc.tensor.matmul(bank[:, 5, HD:2 * HD], pr_t[:, 2 * P:3 * P], v[:, 1, e], start=False,
                                 stop=True).then_inc(pv_done, 1)

            def qk_unit(g):
                o = unit_bank(UNIT[("qk", g)])
                for w in range(2):
                    for t in range(TT):
                        tr = nc.tensor.transpose(o[:, (2 * w + t) * P:(2 * w + t + 1) * P],
                                                 qk[:, t, w, g * P:(g + 1) * P], ident)
                tr.then_inc(tr_done, 1)

            pe.wait_ge(rope_done, 8)
            read_out(pe, 1, U_WIN + 4)
            for j in range(8):
                transposed(UNIT[("mem", j)])
            for k in range(NH):
                pair, c, n = (k // 2) % 2, k // 2, k % 2
                if n == 0:
                    take_pair(pair, U_MKV + c // 2)
                m, j0 = M_MKV + 4 * k, 4 * n
                half(m, j0, pair, 8 * n, x_hi, x_lo, n == 0, False)
                if k:
                    p_unit(k - 1)
                if k % 2 == 0:
                    qk_unit(k // 2)
                half(m + 1, j0 + 1, pair, 8 * n + 2, x_hi, x_lo, False, False)
                if k:
                    weigh(k - 1)
                if k % 2 == 0 and 2 <= k <= 8:
                    read_out(pe, (k // 2 - 1) % 2, U_MKV + (k // 2 - 1) // 2)
                    transpose_unit(UNIT[("mk", k // 2 - 1, 0)], mk_nat, 0)
                half(m + 2, j0 + 2, pair, 8 * n + 4, x_hi, x_lo, False, False)
                scores(k)
                half(m + 3, j0 + 3, pair, 8 * n + 6, x_hi, x_lo, False, n == 1)
                if k % 2 == 0 and 2 <= k <= 8:
                    transpose_unit(UNIT[("mk", k // 2 - 1, 1)], mk_nat, 2)
                if k % 2 and k < 8:
                    if k == 1:
                        pe.wait_ge(sgu_scaled, 2)
                    transpose_unit(UNIT[("sgu", k // 2)], u, 2 * (k // 2))

            mixed = (8, 10, 12, 14, 0, 2, 4, 6)

            def last_head(j):
                if j == 0:
                    p_unit(NH - 1)
                if j == 1:
                    weigh(NH - 1)
                if j == 3:
                    pe.wait_ge(att_scaled, 2)
                    for n in range(4):
                        transpose_unit(UNIT[("att", n)], att, 2 * n)
                if j >= 3 and j < 7:
                    transposed(UNIT[("att", j - 3)])

            def h_units(name, c):
                def after(j):
                    if j in (3, 4):
                        h_unit(name, 2 * c + j - 3)
                return after

            for j in range(4):
                transposed(UNIT[("sgu", j)])
            for c in range(4):
                take_pair(c % 2, U_WO + c // 2)
                square_chunk(M_WO + 8 * c, 0, c % 2, y_hi, y_lo,
                             h_units("h2", c - 1) if c else last_head, mixed)

            def memory_head(c, j):
                if j == 0:
                    read_out(pe, c % 2, U_MQ + c // 2)
                    for n in range(2):
                        transpose_unit(UNIT[("mq", c, n)], mq_nat, 2 * n)
                if j == 1:
                    for n in range(2):
                        transposed(UNIT[("mq", c, n)])
                    if c == 0:
                        for n in range(2):
                            transposed(UNIT[("mk", 3, n)])
                    for t in range(TT):
                        for k in range(4):
                            mm = nc.tensor.matmul(bank[:, 4, t * S:(t + 1) * S], mq_t[:, k, t * P:(t + 1) * P],
                                                  memk_t[:, 4 * c + k, :], start=k == 0, stop=k == 3)
                    mm.then_inc(ms_done, 1)
                if j == 2:
                    o = unit_bank(UNIT[("mp", c)])
                    pe.wait_ge(mp_ready, 2 * c + 2)
                    for b in range(TT):
                        for t in range(TT):
                            tr = nc.tensor.transpose(o[:, (2 * b + t) * P:(2 * b + t + 1) * P],
                                                     mp[:, t, b * P:(b + 1) * P], ident)
                    tr.then_inc(tr_done, 1)
                if j == 3:
                    transposed(UNIT[("mp", c)])
                    if c == 0:
                        read_out(pe, 0, U_MKV + 3)
                        read_out(pe, 1, U_MKV + 3)
                    for t in range(TT):
                        if c or t:
                            pe.wait_ge(mo_ready, 2 * c + t)
                        for b in range(TT):
                            mm = nc.tensor.matmul(bank[:, 5, :], mp_t[:, b, t * P:(t + 1) * P],
                                                  memv[:, b, c * MHD:(c + 1) * MHD], start=b == 0, stop=b == 1)
                        mm.then_inc(mpv_done, 1)
                if j == 5:
                    pe.wait_ge(mo_ready, 2 * c + 2)
                    for n in range(2):
                        transpose_unit(UNIT[("o", c, n)], mo_nat, 2 * n)

            for j in range(6):
                transposed(UNIT[("h2", j)])
            last_h2 = last_h_units("h2")
            for c in range(4):
                take_pair(c % 2, U_MQ + c // 2)
                square_chunk(M_MQ + 8 * c, 0, c % 2, x_hi, x_lo,
                             (lambda j, c=c: memory_head(c - 1, j)) if c else last_h2)

            def last_memory_head(j):
                memory_head(3, j)
                if j == 5:
                    transposed(UNIT[("o", 3, 0)])
                    transposed(UNIT[("o", 3, 1)])

            for c in range(3):
                for n in range(2):
                    transposed(UNIT[("o", c, n)])
            for c in range(4):
                take_pair(c % 2, U_MO + c // 2)
                square_chunk(M_MO + 8 * c, 0, c % 2, y_hi, y_lo,
                             h_units("h3", c - 1) if c else last_memory_head)

            for j in range(6):
                transposed(UNIT[("h3", j)])
            last_h3 = last_h_units("h3")
            ffn(M_F2, U_F2, 2 * FCH, "a2", lambda j: last_h3(j - 1), lambda c: None)

        @block.scalar
        def _(act):
            def split(m, j):
                if isinstance(m, int) and m >= M_END:
                    return
                slot, n = (j // 2) % RAW, j % 2
                if n == 0:
                    act.wait_ge(landed[slot], (m - j) * 2 + 16 * (j // 8 + 1))
                if not isinstance(m, int) or m >= RING:
                    act.wait_ge(half_used, m - RING + 1)
                nc.scalar.activation(w_hi[:, j % RING, :, :], raw[:, slot, 2 * n:2 * n + 2, :],
                                     ACT.Copy).then_inc(hi_ready, 1)

            def splits(m, j, count):
                for n in range(count):
                    split(m + (AHEAD + n), j + AHEAD + n)

            def read_unit_hi(n, dst_hi, kt, gain=None):
                act.wait_ge(tr_done, n + 1)
                src = bank[:, 6 + n % 2, :].rearrange("p (k s) -> p k s", k=2)
                if gain is None:
                    nc.scalar.activation(dst_hi[:, kt:kt + 2, :], src, ACT.Copy).then_inc(tr_hi, 1)
                else:
                    for k in range(2):
                        op = nc.scalar.activation(dst_hi[:, kt + k, :], src[:, k, :], ACT.Copy,
                                                  scale=cols[:, gain + k:gain + k + 1])
                    op.then_inc(tr_hi, 1)

            def read_unit(n, dst, width=NC):
                act.wait_ge(tr_done, n + 1)
                nc.scalar.activation(dst, bank[:, 6 + n % 2, 0:width], ACT.Copy).then_inc(tr_free[n % 2], 1)

            squares_done = [0]

            def squares(src, acc):
                if squares_done[0]:
                    act.wait_ge(squared, squares_done[0])
                squares_done[0] += 1
                nc.scalar.activation(junk[:, 0:src.shape[1]], src, ACT.Square,
                                     accum_out=acc).then_inc(squared, 1)

            def h_squares(name, c):
                for t in range(TT):
                    read_out(act, *final[name][c], t)
                    squares(h[:, t, c * NC:(c + 1) * NC], ssq[:, t, c:c + 1])

            roots = [0]

            def square_root():
                roots[0] += 1
                act.wait_ge(var_ready, roots[0])
                nc.scalar.activation(root, var, ACT.Sqrt).then_inc(root_ready, 1)

            def ffn(m0, name, uses, before, last_units, h_name):
                n = before()
                splits(m0 + n, n, 8 - n)
                act.wait_ge(rstd_ready, {"a1": 1, "a2": 8}[name])
                act.wait_ge(half_used, m0 + 8)
                for t in range(TT):
                    nc.scalar.activation(silu[:, t, :], pair_bank(0, t), ACT.Silu,
                                         scale=rstd[:, t:t + 1]).then_inc(pair_free[0], 1)
                splits(m0 + 8, 8, 8)
                n0_ = UNIT[(name, 0, 0)]
                with act.Fori(0, FCH - 1) as i:
                    m = i * 24 + (m0 + 16)
                    splits(m, 0, 8)
                    act.wait_ge(half_used, m + 8)
                    act.wait_ge(pair_free[1], i * 4 + (2 * uses + 2))
                    for t in range(TT):
                        nc.scalar.activation(silu[:, t, :], pair_bank(0, t), ACT.Silu,
                                             scale=rstd[:, t:t + 1]).then_inc(pair_free[0], 1)
                    for n in range(2):
                        act.wait_ge(tr_done, i * 2 + (n0_ + n + 1))
                        nc.scalar.activation(aT_hi[:, 2 * n:2 * n + 2, :],
                                             bank[:, 6 + (n0_ + n) % 2, :].rearrange("p (k s) -> p k s", k=2),
                                             ACT.Copy).then_inc(tr_hi, 1)
                    splits(m + 8, 8, 16)
                for n in range(2):
                    read_unit_hi(UNIT[(name, FCH - 1, n)], aT_hi, 2 * n)
                m = m0 + FFN_HALVES - 8
                for c in range(4):
                    splits(m + 2 * c, 2 * c, 2)
                    h_squares(h_name, c)
                    last_units(c)

            act.dma_start(vec_rows[0:KT, :], a["ffn1_norm"].rearrange("(r c) -> r c", c=P)).then_inc(vec_in, 16)
            act.dma_start(const[:, :], a["const"]).then_inc(const_in, 16)
            for c in range(4):
                act.dma_start(h[:, :, c * NC:(c + 1) * NC],
                              a["x"][:, c * NC:(c + 1) * NC].rearrange("(t p) n -> p t n", p=P)).then_inc(x_in[c], 16)
            for at, name in ((G_MIX, "mix_norm"), (G_MEMQ, "mem_q_norm"), (G_MEMKV, "mem_kv_norm"),
                             (G_FFN2, "ffn2_norm"), (G_ATTN, "attn_out_gain"), (G_SGU, "sgu_out_gain")):
                src = a[name].rearrange("(r c) -> r c", c=P)
                act.dma_start(vec_rows[at:at + src.shape[0], :], src).then_inc(vec_in, 16)
            act.dma_start(vec_rows[B_SGU:B_SGU + NG, :], a["sgu_b_s"]).then_inc(vec_in, 16)
            act.dma_start(ws_nat, a["sgu_w_s"].rearrange("g i j -> i g j")).then_inc(ws_in, 16)
            with nc.allow_non_contiguous_dma(reason="256 positions, one per partition and tile"):
                act.dma_start(pos[:, :], a["positions"].rearrange("(t p) -> p t", p=P)).then_inc(pos_in, 16)
            act.dma_start(ln_gain, a["sgu_ln_gain"].partition_broadcast(P)).then_inc(ln_in, 16)
            act.dma_start(ln_bias, a["sgu_ln_bias"].partition_broadcast(P)).then_inc(ln_in, 16)
            act.dma_start(mem_nat, a["mem"].rearrange("(t p) n -> p t n", p=P)).then_inc(mem_in, 16)

            act.wait_ge(tr_done, UNIT[("cols",)] + 1)
            n = UNIT[("cols",)]
            nc.scalar.activation(cols[:, :], bank[:, 6 + n % 2, 0:NVEC], ACT.Copy).then_inc(tr_free[n % 2], 1)
            act.wait_ge(tr_free[n % 2], n // 2 + 1)

            def first_splits():
                for j in range(8):
                    if j < AHEAD + 2:
                        split(j, j)
                    read_unit_hi(UNIT[("x", j)], x_hi, 2 * j, G_FFN1 + 2 * j)
                for c in range(4):
                    for t in range(TT):
                        act.wait_ge(x_in[c], 16)
                        squares(h[:, t, c * NC:(c + 1) * NC], ssq[:, t, c:c + 1])
                square_root()
                return 2

            def h1_units(c):
                if c:
                    for j in (2 * c - 2, 2 * c - 1):
                        read_unit_hi(UNIT[("h1", j)], y_hi, 2 * j, G_MIX + 2 * j)

            ffn(M_F1, "a1", U_F1, first_splits, h1_units, "h1")

            square_root()
            act.wait_ge(rstd_ready, 2)
            splits(M_WIN, 0, 2)
            for j in (6, 7):
                read_unit_hi(UNIT[("h1", j)], y_hi, 2 * j, G_MIX + 2 * j)
            splits(M_WIN + 2, 2, 2)
            read_unit(UNIT[("ws", 0)], ws_t[:, 0:4, :].rearrange("p g i -> p (g i)"))
            splits(M_WIN + 4, 4, 1)
            read_unit(UNIT[("ws", 1)], ws_t[:, 4:8, :].rearrange("p g i -> p (g i)"))
            splits(M_WIN + 5, 5, 3)

            def tiles(dst, c):
                return [dst[:, t, c * NC:(c + 1) * NC] for t in range(TT)]

            m = M_WIN
            for c in range(2):
                if c:
                    splits(m + 8, 8, 8)
                act.wait_ge(half_used, m + 8 * c + 8)
                for t in range(TT):
                    nc.scalar.activation(tiles(gv, c)[t], pair_bank(c, t), ACT.Gelu_apprx_tanh,
                                         scale=rstd[:, t:t + 1], accum_out=gv_sum[:, t, c:c + 1])\
                        .then_inc(pair_free[c], 1)
            m = M_WIN + 16
            for c in range(2):
                splits(m + 8 * c, 8 * c, 6)
                if c == 0:
                    for t in range(TT):
                        act.wait_ge(centred, t + 1)
                        for b in range(2):
                            squares(tiles(gv, b)[t], gv_ssq[:, t, b:b + 1])
                else:
                    square_root()
                splits(m + 8 * c + 6, 8 * c + 6, 2)
                act.wait_ge(half_used, m + 8 * c + 8)
                for t in range(TT):
                    nc.scalar.activation(tiles(u, c)[t], pair_bank(c, t), ACT.Gelu_apprx_tanh,
                                         scale=rstd[:, t:t + 1]).then_inc(pair_free[c], 1)
            for w in range(2):
                m = M_WIN + 32 + 16 * w
                for c in range(2):
                    splits(m + 8 * c, 8 * c, 4)
                    if w == 1 and c == 0:
                        square_root()
                    splits(m + 8 * c + 4, 8 * c + 4, 4)
                    act.wait_ge(half_used, m + 8 * c + 8)
                    for t in range(TT):
                        nc.scalar.activation(qk[:, t, w, c * NC:(c + 1) * NC], pair_bank(c, t), ACT.Copy,
                                             scale=rstd[:, t:t + 1]).then_inc(pair_free[c], 1)
                    if w == 0 and c == 0:
                        act.wait_ge(trig_arg, 1)
                        nc.scalar.activation(trig[:, :, :, :], trig[:, :, :, :], ACT.Sin).then_inc(trig_ready, 1)
                    if w == 0 and c == 1:
                        act.wait_ge(mem_in, 16)
                        for t in range(TT):
                            for b in range(4):
                                squares(mem_nat[:, t, b * NC:(b + 1) * NC], mem_ssq[:, t, b:b + 1])
            m = M_WIN + 64
            for j in range(8):
                splits(m + j, j, 1)
                read_unit_hi(UNIT[("mem", j)], x_hi, 2 * j, G_MEMKV + 2 * j)
            for c in range(2):
                if c:
                    splits(m + 8, 8, 8)
                act.wait_ge(half_used, m + 8 * c + 8)
                for t in range(TT):
                    nc.scalar.activation(v[:, t, c * NC:(c + 1) * NC], pair_bank(c, t), ACT.Copy,
                                         scale=rstd[:, t:t + 1]).then_inc(pair_free[c], 1)

            def exponentials(k):
                act.wait_ge(s_masked, k + 1)
                if k:
                    act.wait_ge(tr_done, UNIT[("p", k - 1)] + 1)
                nc.scalar.activation(pr[:, 0:P], sm[:, 0:P], ACT.Exp, bias=s_neg[:, 0:1], scale=ATT_SCALE,
                                     accum_out=s_sum[:, 0:1])
                nc.scalar.activation(pr[:, P:3 * P], sm[:, P:3 * P], ACT.Exp, bias=s_neg[:, 1:2], scale=ATT_SCALE,
                                     accum_out=s_sum[:, 1:2]).then_inc(p_ready, 1)

            def att_squares(g):
                act.wait_ge(o_ready, 4 * g + 4)
                for t in range(TT):
                    squares(att[:, t, 256 * g:256 * g + 256], att_ssq[:, t, g:g + 1])

            act.wait_ge(rstd_ready, 4)
            for k in range(NH):
                m, n, c = M_MKV + 4 * k, k % 2, k // 2
                splits(m, 4 * n, 1)
                if k:
                    read_unit(UNIT[("p", k - 1)], pr_t, 3 * P)
                if k % 2 == 0:
                    read_unit(UNIT[("qk", k // 2)], qk_t)
                splits(m + 1, 4 * n + 1, 1)
                if k % 2 == 0 and 2 <= k <= 8:
                    b = k // 2 - 1
                    read_unit(UNIT[("mk", b, 0)], memk_t[:, 4 * b:4 * b + 2, :].rearrange("p k s -> p (k s)"))
                splits(m + 2, 4 * n + 2, 1)
                if k == 0:
                    act.wait_ge(sgu_ready, 16)
                    for t in range(TT):
                        for b in range(2):
                            squares(tiles(u, b)[t], sgu_ssq[:, t, b:b + 1])
                    square_root()
                splits(m + 3, 4 * n + 3, 1)
                if k % 2 == 0 and 2 <= k <= 8:
                    read_unit(UNIT[("mk", b, 1)], memk_t[:, 4 * b + 2:4 * b + 4, :].rearrange("p k s -> p (k s)"))
                if k % 2 and k < 8:
                    read_unit_hi(UNIT[("sgu", k // 2)], y_hi, 8 + 2 * (k // 2), G_SGU + 2 * (k // 2))
                exponentials(k)
                if n == 1:
                    act.wait_ge(half_used, m + 4)
                    for t in range(TT):
                        dst = mk_nat[:, t, :] if c < 4 else memv[:, t, (c - 4) * NC:(c - 3) * NC]
                        nc.scalar.activation(dst, pair_bank(c % 2, t), ACT.Copy,
                                             scale=mem_rstd[:, t:t + 1]).then_inc(pair_free[c % 2], 1)
                if k in (5, 9, 13):
                    att_squares(k // 4 - 1)

            for c in range(4):
                m = M_WO + 8 * c
                if c == 0:
                    splits(m, 0, 1)
                    read_unit(UNIT[("p", NH - 1)], pr_t, 3 * P)
                    splits(m + 1, 1, 1)
                    att_squares(3)
                    splits(m + 2, 2, 1)
                    square_root()
                    splits(m + 3, 3, 1)
                    for j in range(4):
                        read_unit_hi(UNIT[("att", j)], y_hi, 2 * j, G_ATTN + 2 * j)
                    splits(m + 4, 4, 4)
                else:
                    splits(m, 0, 5)
                    for j in (2 * c - 2, 2 * c - 1):
                        read_unit_hi(UNIT[("h2", j)], x_hi, 2 * j, G_MEMQ + 2 * j)
                    h_squares("h2", c - 1)
                    splits(m + 5, 5, 3)

            def memory_head(c, m, j0):
                splits(m, j0, 1)
                for n in range(2):
                    read_unit(UNIT[("mq", c, n)], mq_t[:, 2 * n:2 * n + 2, :].rearrange("p k s -> p (k s)"))
                splits(m + 1, j0 + 1, 1)
                act.wait_ge(mmax_ready, c + 1)
                for t in range(TT):
                    nc.scalar.activation(mp[:, t, :], bank[:, 4, t * S:(t + 1) * S], ACT.Exp, bias=s_neg[:, t:t + 1],
                                         scale=MEM_SCALE, accum_out=s_sum[:, t:t + 1]).then_inc(mp_ready, 1)
                splits(m + 2, j0 + 2, 1)
                read_unit(UNIT[("mp", c)], mp_t.rearrange("p m q -> p (m q)"))
                splits(m + 3, j0 + 3, 3)
                for n in range(2):
                    read_unit_hi(UNIT[("o", c, n)], y_hi, 4 * c + 2 * n)
                splits(m + 6, j0 + 6, 2)

            for c in range(4):
                m = M_MQ + 8 * c
                if c == 0:
                    splits(m, 0, 2)
                    for j in (6, 7):
                        read_unit_hi(UNIT[("h2", j)], x_hi, 2 * j, G_MEMQ + 2 * j)
                    h_squares("h2", 3)
                    square_root()
                    act.wait_ge(rstd_ready, 7)
                    splits(m + 2, 2, 6)
                else:
                    memory_head(c - 1, m, 0)
                act.wait_ge(half_used, m + 8)
                for t in range(TT):
                    nc.scalar.activation(mq_nat[:, t, :], pair_bank(c % 2, t), ACT.Copy,
                                         scale=rstd[:, t:t + 1]).then_inc(pair_free[c % 2], 1)
            for c in range(4):
                m = M_MO + 8 * c
                if c == 0:
                    memory_head(3, m, 0)
                else:
                    splits(m, 0, 5)
                    for j in (2 * c - 2, 2 * c - 1):
                        read_unit_hi(UNIT[("h3", j)], x_hi, 2 * j, G_FFN2 + 2 * j)
                    h_squares("h3", c - 1)
                    splits(m + 5, 5, 3)

            def last_h3():
                splits(M_F2, 0, 2)
                for j in (6, 7):
                    read_unit_hi(UNIT[("h3", j)], x_hi, 2 * j, G_FFN2 + 2 * j)
                h_squares("h3", 3)
                square_root()
                return 2

            act.dma_start(final_gain, a["final_norm"].partition_broadcast(P)).then_inc(gain_in, 16)
            ffn(M_F2, "a2", U_F2, last_h3, lambda c: None, "h4")
            square_root()

        @block.vector
        def _(dve):
            steps = [0]

            def link(ins):
                steps[0] += 1
                ins.then_inc(step, 1)
                dve.wait_ge(step, steps[0])

            def split(m, j):
                if isinstance(m, int) and m >= M_END:
                    return
                slot, n = (j // 2) % RAW, j % 2
                dve.wait_ge(hi_ready, m + 1)
                nc.vector.tensor_tensor(w_lo[:, j % RING, :, :], raw[:, slot, 2 * n:2 * n + 2, :],
                                        f32(w_hi[:, j % RING, :, :]), ALU.subtract).then_inc(lo_ready, 1)

            def splits(m, j, count):
                for n in range(count):
                    split(m + (AHEAD + n), j + AHEAD + n)

            def read_unit_lo(name, dst_hi, dst_lo, kt, gain=None):
                n = UNIT[name]
                dve.wait_ge(tr_hi, SPLIT[name] + 1)
                src = bank[:, 6 + n % 2, :].rearrange("p (k s) -> p k s", k=2)
                if gain is None:
                    nc.vector.tensor_tensor(dst_lo[:, kt:kt + 2, :], src, f32(dst_hi[:, kt:kt + 2, :]),
                                            ALU.subtract).then_inc(tr_free[n % 2], 1)
                else:
                    for k in range(2):
                        op = nc.vector.scalar_tensor_tensor(
                            dst_lo[:, kt + k, :], src[:, k, :], cols[:, gain + k:gain + k + 1],
                            f32(dst_hi[:, kt + k, :]), ALU.mult, ALU.subtract)
                    op.then_inc(tr_free[n % 2], 1)

            counts = {"squared": 0, "root": 0}

            def inverse_rms(acc, width, dst, parts):
                counts["squared"] += TT * parts
                dve.wait_ge(squared, counts["squared"])
                link(nc.vector.tensor_reduce(n0, acc, AX_X, ALU.add))
                nc.vector.tensor_scalar(var, n0, 1.0 / width, EPS, ALU.mult, ALU.add).then_inc(var_ready, 1)
                counts["root"] += 1
                dve.wait_ge(var_ready, counts["root"])
                dve.wait_ge(root_ready, counts["root"])
                link(nc.vector.reciprocal(n1, root))
                link(nc.vector.tensor_tensor(n1, n1, var, ALU.mult))
                link(nc.vector.tensor_tensor(n1, n1, root, ALU.add))
                link(nc.vector.tensor_scalar(n1, n1, 0.5, None, ALU.mult))
                nc.vector.reciprocal(dst, n1).then_inc(rstd_ready, 1)
                dve.wait_ge(rstd_ready, counts["root"])

            def add_to_h(m_done, pair, c, scale):
                dve.wait_ge(half_used, m_done)
                for t in range(TT):
                    hc = h[:, t, c * NC:(c + 1) * NC]
                    op = nc.vector.scalar_tensor_tensor(hc, pair_bank(pair, t), scale, hc, ALU.mult, ALU.add)
                    op.then_inc(pair_free[pair], 1)

            def ffn(m0, name, before, last_units):
                def hidden(m_done):
                    dve.wait_ge(half_used, m_done)
                    for t in range(TT):
                        nc.vector.scalar_tensor_tensor(hid[:, t, :], pair_bank(1, t), rstd[:, t:t + 1],
                                                       silu[:, t, :], ALU.mult, ALU.mult).then_inc(pair_free[1], 1)

                n = before()
                splits(m0 + n, n, 16 - n)
                dve.wait_ge(pair_free[0], {"a1": 2, "a2": 2 * U_F2 + 2}[name])
                hidden(m0 + 16)
                base = {"a1": U_F1, "a2": U_F2}[name]
                base2 = {"a1": 0, "a2": 2 * FCH}[name]
                n0_, v0 = UNIT[(name, 0, 0)], SPLIT[(name, 0, 0)]
                with dve.Fori(0, FCH - 1) as i:
                    m = i * 24 + (m0 + 16)
                    splits(m, 0, 8)
                    for n in range(2):
                        dve.wait_ge(tr_hi, i * 2 + (v0 + n + 1))
                        nc.vector.tensor_tensor(
                            aT_lo[:, 2 * n:2 * n + 2, :],
                            bank[:, 6 + (n0_ + n) % 2, :].rearrange("p (k s) -> p k s", k=2),
                            f32(aT_hi[:, 2 * n:2 * n + 2, :]), ALU.subtract).then_inc(tr_free[(n0_ + n) % 2], 1)
                    splits(m + 8, 8, 8)
                    dve.wait_ge(pair_free[0], i * 4 + (2 * base + 4))
                    hidden(m + 16)
                    for c, pair in enumerate((2, 0, 2, 1)):
                        splits(m + 16 + 2 * c, 16 + 2 * c, 2)
                        dve.wait_ge(half_used, m + (16 + 2 * c + 2))
                        for t in range(TT):
                            hc = h[:, t, c * NC:(c + 1) * NC]
                            nc.vector.scalar_tensor_tensor(hc, pair_bank(pair, t), 0.5, hc, ALU.mult,
                                                           ALU.add).then_inc(pair_free[pair], 1)
                for n in range(2):
                    read_unit_lo((name, FCH - 1, n), aT_hi, aT_lo, 2 * n)
                m = m0 + FFN_HALVES - 8
                for c, pair in enumerate((2, 0, 2, 1)):
                    splits(m + 2 * c, 2 * c, 2)
                    add_to_h(m + 2 * c + 2, pair, c, 0.5)
                    last_units(c)

            def first_splits():
                for j in range(8):
                    if j < AHEAD + 2:
                        split(j, j)
                    if j == 0:
                        dve.wait_ge(tr_free[0], 1)
                    read_unit_lo(("x", j), x_hi, x_lo, 2 * j, G_FFN1 + 2 * j)
                inverse_rms(ssq, D, rstd, 4)
                return 2

            def h1_units(c):
                if c:
                    for j in (2 * c - 2, 2 * c - 1):
                        read_unit_lo(("h1", j), y_hi, y_lo, 2 * j, G_MIX + 2 * j)

            ffn(M_F1, "a1", first_splits, h1_units)
            inverse_rms(ssq, D, rstd, 4)

            def angles():
                two_pi = 2 * np.pi
                magic = 1.5 * 2.0 ** 23

                def part(x, grid):
                    return float(np.round(x / grid) * grid)

                def parts(x):
                    p1 = part(x, 2.0 ** -10)
                    p2 = part(x - p1, 2.0 ** -22)
                    return p1, p2, float(np.float32(x - p1 - p2))

                c20 = parts(float(np.remainder(2.0 ** 20 + np.pi, two_pi) - np.pi))
                c10 = parts(float(np.remainder(2.0 ** 10 + np.pi, two_pi) - np.pi))
                cp = parts(two_pi)
                flat = [rope_tmp[:, r, 0:64] for r in range(4)]
                rest, n2, n1, n0_ = flat
                lowp = rope_tmp[:, 0, 64:128]
                posf = stat[:, 66:68]
                dve.wait_ge(pos_in, 16)
                dve.wait_ge(const_in, 16)
                link(nc.vector.tensor_copy(posf, pos[:, :]))
                for t in range(TT):
                    link(nc.vector.tensor_scalar(rest[:, 32 * t:32 * t + 32], const[:, C_FREQ:C_FREQ + 32],
                                                 posf[:, t:t + 1], None, ALU.mult))
                for dst, size in ((n2, 2.0 ** 20), (n1, 2.0 ** 10)):
                    link(nc.vector.tensor_scalar(dst, rest, 1 / size, magic, ALU.mult, ALU.add))
                    link(nc.vector.tensor_scalar(dst, dst, -magic, None, ALU.add))
                    link(nc.vector.scalar_tensor_tensor(rest, dst, -size, rest, ALU.mult, ALU.add))
                link(nc.vector.scalar_tensor_tensor(rest, n2, c20[0], rest, ALU.mult, ALU.add))
                link(nc.vector.scalar_tensor_tensor(rest, n1, c10[0], rest, ALU.mult, ALU.add))
                link(nc.vector.tensor_scalar(n0_, rest, 1 / two_pi, magic, ALU.mult, ALU.add))
                link(nc.vector.tensor_scalar(n0_, n0_, -magic, None, ALU.add))
                link(nc.vector.scalar_tensor_tensor(rest, n0_, -cp[0], rest, ALU.mult, ALU.add))
                link(nc.vector.tensor_scalar(lowp, n2, c20[1], None, ALU.mult))
                link(nc.vector.scalar_tensor_tensor(lowp, n1, c10[1], lowp, ALU.mult, ALU.add))
                link(nc.vector.scalar_tensor_tensor(lowp, n0_, -cp[1], lowp, ALU.mult, ALU.add))
                link(nc.vector.tensor_tensor(rest, rest, lowp, ALU.add))
                link(nc.vector.scalar_tensor_tensor(rest, n2, c20[2], rest, ALU.mult, ALU.add))
                link(nc.vector.scalar_tensor_tensor(rest, n1, c10[2], rest, ALU.mult, ALU.add))
                link(nc.vector.scalar_tensor_tensor(rest, n0_, -cp[2], rest, ALU.mult, ALU.add))
                link(nc.vector.tensor_scalar(n0_, rest, 1 / two_pi, magic, ALU.mult, ALU.add))
                link(nc.vector.tensor_scalar(n0_, n0_, -magic, None, ALU.add))
                link(nc.vector.scalar_tensor_tensor(rest, n0_, -float(np.float32(two_pi)), rest, ALU.mult, ALU.add))
                lim = float(np.nextafter(np.float32(np.pi), np.float32(0)))
                sin_arg = trig[:, 1, :, :].rearrange("p t f -> p (t f)")
                cos_arg = trig[:, 0, :, :].rearrange("p t f -> p (t f)")
                link(nc.vector.tensor_scalar(sin_arg, rest, lim, -lim, ALU.min, ALU.max))
                link(nc.vector.tensor_scalar(n0_, sin_arg, -1.0, None, ALU.mult))
                link(nc.vector.tensor_tensor(n0_, n0_, sin_arg, ALU.max))
                nc.vector.tensor_scalar(cos_arg, n0_, -1.0, float(np.pi / 2), ALU.mult, ALU.add)\
                    .then_inc(trig_arg, 1)

            splits(M_WIN, 0, 2)
            for j in (6, 7):
                read_unit_lo(("h1", j), y_hi, y_lo, 2 * j, G_MIX + 2 * j)
            splits(M_WIN + 2, 2, 6)
            splits(M_WIN + 8, 8, 8)

            m = M_WIN + 16
            splits(m, 0, 4)
            read_out(dve, 0, U_WIN)
            read_out(dve, 1, U_WIN)
            link(nc.vector.tensor_reduce(gv_mean, gv_sum, AX_X, ALU.add))
            link(nc.vector.tensor_scalar(gv_mean, gv_mean, 1.0 / AW, None, ALU.mult))
            for t in range(TT):
                nc.vector.tensor_scalar(gv[:, t, :], gv[:, t, :], gv_mean[:, t:t + 1], None,
                                        ALU.subtract).then_inc(centred, 1)
            splits(m + 4, 4, 8)
            inverse_rms(gv_ssq, AW, gv_rstd, 2)
            dve.wait_ge(ln_in, 32)
            for t in range(TT):
                link(nc.vector.scalar_tensor_tensor(gv[:, t, :], gv[:, t, :], gv_rstd[:, t:t + 1], ln_gain,
                                                    ALU.mult, ALU.mult))
                nc.vector.tensor_tensor(gv[:, t, :], gv[:, t, :], ln_bias, ALU.add).then_inc(gv_ready, 1)
            splits(m + 12, 12, 4)

            def rotate(w, c):
                r4 = [rope_tmp[:, r, :].rearrange("p (e n) -> p e n", n=32) for r in range(4)]
                read_out(dve, c, U_WIN + 2 + w)
                for t in range(TT):
                    x4 = qk[:, t, w, c * NC:(c + 1) * NC].rearrange("p (e n) -> p e n", n=HD)
                    x1, x2 = x4[:, :, 0:32], x4[:, :, 32:64]
                    cos, sin = (trig[:, r, t, :].unsqueeze(1).to_broadcast([P, 8, 32]) for r in range(2))
                    nc.vector.tensor_tensor(r4[0], x1, cos, ALU.mult)
                    nc.vector.tensor_tensor(r4[1], x2, sin, ALU.mult)
                    nc.vector.tensor_tensor(r4[2], x1, sin, ALU.mult)
                    link(nc.vector.tensor_tensor(r4[3], x2, cos, ALU.mult))
                    nc.vector.tensor_tensor(x1, r4[0], r4[1], ALU.subtract)
                    nc.vector.tensor_tensor(x2, r4[2], r4[3], ALU.add).then_inc(rope_done, 1)
                    dve.wait_ge(rope_done, 4 * w + 2 * c + t + 1)

            m = M_WIN + 32
            splits(m, 0, 4)
            angles()
            splits(m + 4, 4, 8)
            dve.wait_ge(trig_ready, 1)
            rotate(0, 0)
            splits(m + 12, 12, 4)
            m = M_WIN + 48
            splits(m, 0, 4)
            rotate(0, 1)
            inverse_rms(mem_ssq, D, mem_rstd, 4)
            splits(m + 4, 4, 8)
            rotate(1, 0)
            splits(m + 12, 12, 4)
            m = M_WIN + 64
            for j in range(8):
                splits(m + j, j, 1)
                read_unit_lo(("mem", j), x_hi, x_lo, 2 * j, G_MEMKV + 2 * j)
                if j == 1:
                    rotate(1, 1)
            for j in range(8, 16):
                splits(m + j, j, 1)
                if j % 2 and 8 < j < 16:
                    b = (j - 9) // 2
                    t, n = b // 2, b % 2
                    dve.wait_ge(sv_done, b + 1)
                    read_out(dve, 1, U_WIN + 1)
                    for g in range(4):
                        gg = 4 * n + g
                        ug = u[:, t, gg * P:(gg + 1) * P]
                        nc.vector.scalar_tensor_tensor(ug, bank[:, 4 + n, g * P:(g + 1) * P],
                                                       cols[:, B_SGU + gg:B_SGU + gg + 1], ug, ALU.add,
                                                       ALU.mult).then_inc(sgu_ready, 1)

            def mask_scores(k):
                dve.wait_ge(s_done, k + 1)
                if k:
                    dve.wait_ge(p_ready, k)
                for t, (lo, hi) in enumerate(((0, P), (P, 3 * P))):
                    op = nc.vector.tensor_tensor_reduce(
                        out=sm[:, lo:hi], in0=bank[:, 4, lo:hi], in1=const[:, C_MASK + lo:C_MASK + hi],
                        scale=1.0, scalar=-3e38, op0=ALU.add, op1=ALU.max, accum_out=s_max[:, t:t + 1])
                link(op)
                nc.vector.tensor_scalar(s_neg, s_max, -ATT_SCALE, None, ALU.mult).then_inc(s_masked, 1)

            def head_out(k):
                link(nc.vector.reciprocal(s_inv, s_sum))
                dve.wait_ge(pv_done, k + 1)
                for t in range(TT):
                    op = nc.vector.tensor_scalar(att[:, t, HD * k:HD * k + HD], bank[:, 5, HD * t:HD * t + HD],
                                                 s_inv[:, t:t + 1], None, ALU.mult)
                op.then_inc(o_ready, 1)

            def scale_tiles(src, factor, done):
                for t in range(TT):
                    nc.vector.tensor_scalar(src[:, t, :], src[:, t, :], factor[:, t:t + 1], None,
                                            ALU.mult).then_inc(done, 1)

            for k in range(NH):
                m, n = M_MKV + 4 * k, k % 2
                splits(m, 4 * n, 2)
                if k:
                    head_out(k - 1)
                splits(m + 2, 4 * n + 2, 1)
                mask_scores(k)
                if k == 0:
                    inverse_rms(sgu_ssq, AW, sgu_rstd, 2)
                    scale_tiles(u, sgu_rstd, sgu_scaled)
                splits(m + 3, 4 * n + 3, 1)
                if k % 2 and k < 8:
                    read_unit_lo(("sgu", k // 2), y_hi, y_lo, 8 + 2 * (k // 2), G_SGU + 2 * (k // 2))

            for c in range(4):
                m = M_WO + 8 * c
                if c == 0:
                    splits(m, 0, 2)
                    head_out(NH - 1)
                    splits(m + 2, 2, 1)
                    inverse_rms(att_ssq, AW, att_rstd, 4)
                    scale_tiles(att, att_rstd, att_scaled)
                    splits(m + 3, 3, 1)
                    for j in range(4):
                        read_unit_lo(("att", j), y_hi, y_lo, 2 * j, G_ATTN + 2 * j)
                    splits(m + 4, 4, 4)
                else:
                    splits(m, 0, 5)
                    for j in (2 * c - 2, 2 * c - 1):
                        read_unit_lo(("h2", j), x_hi, x_lo, 2 * j, G_MEMQ + 2 * j)
                    splits(m + 5, 5, 3)
                add_to_h(m + 8, c % 2, c, 1.0)

            def memory_head(c, m, j0):
                splits(m, j0, 2)
                dve.wait_ge(ms_done, c + 1)
                link(nc.vector.tensor_reduce(s_max, bank[:, 4, :].rearrange("p (t m) -> p t m", t=TT), AX_X, ALU.max))
                nc.vector.tensor_scalar(s_neg, s_max, -MEM_SCALE, None, ALU.mult).then_inc(mmax_ready, 1)
                splits(m + 2, j0 + 2, 2)
                dve.wait_ge(mp_ready, 2 * c + 2)
                link(nc.vector.reciprocal(s_inv, s_sum))
                for t in range(TT):
                    dve.wait_ge(mpv_done, 2 * c + t + 1)
                    nc.vector.tensor_scalar(mo_nat[:, t, :], bank[:, 5, :], s_inv[:, t:t + 1], None,
                                            ALU.mult).then_inc(mo_ready, 1)
                splits(m + 4, j0 + 4, 2)
                for n in range(2):
                    read_unit_lo(("o", c, n), y_hi, y_lo, 4 * c + 2 * n)
                splits(m + 6, j0 + 6, 2)

            for c in range(4):
                m = M_MQ + 8 * c
                if c == 0:
                    splits(m, 0, 2)
                    for j in (6, 7):
                        read_unit_lo(("h2", j), x_hi, x_lo, 2 * j, G_MEMQ + 2 * j)
                    inverse_rms(ssq, D, rstd, 4)
                    splits(m + 2, 2, 6)
                else:
                    memory_head(c - 1, m, 0)
            for c in range(4):
                m = M_MO + 8 * c
                if c == 0:
                    memory_head(3, m, 0)
                else:
                    splits(m, 0, 5)
                    for j in (2 * c - 2, 2 * c - 1):
                        read_unit_lo(("h3", j), x_hi, x_lo, 2 * j, G_FFN2 + 2 * j)
                    splits(m + 5, 5, 3)
                add_to_h(m + 8, c % 2, c, 1.0)

            def last_h3():
                splits(M_F2, 0, 2)
                for j in (6, 7):
                    read_unit_lo(("h3", j), x_hi, x_lo, 2 * j, G_FFN2 + 2 * j)
                inverse_rms(ssq, D, rstd, 4)
                return 2

            ffn(M_F2, "a2", last_h3, lambda c: None)

            inverse_rms(ssq, D, rstd, 4)
            dve.wait_ge(gain_in, 16)
            for t in range(TT):
                for c in range(2):
                    e = slice(c * AW, (c + 1) * AW)
                    nc.vector.scalar_tensor_tensor(y_out[:, t, e], h[:, t, e], rstd[:, t:t + 1],
                                                   final_gain[:, e], ALU.mult, ALU.mult).then_inc(y_ready, 1)


_NAMES = ("x", "mem", "positions", "ffn1_norm", "ffn1_w_gate", "ffn1_w_up", "ffn1_w_down", "mix_norm", "w_in",
          "sgu_ln_gain", "sgu_ln_bias", "sgu_w_s", "sgu_b_s", "attn_out_gain", "sgu_out_gain", "w_out",
          "mem_q_norm", "mem_kv_norm", "mem_w_q", "mem_w_k", "mem_w_v", "mem_w_o", "ffn2_norm",
          "ffn2_w_gate", "ffn2_w_up", "ffn2_w_down")


def shape_constants():
    const = np.zeros((P, C_END), np.float32)
    const[:, C_ID:C_ID + P] = np.eye(P, dtype=np.float32)
    i = np.arange(P)[:, None]
    for col, diff in ((C_MASK, i - np.arange(P)[None]), (C_MASK + P, i + P - np.arange(2 * P)[None])):
        count = np.zeros(diff.shape)
        for window, dilation in ((128, 1), (512, 4), (2048, 16)):
            count += (diff >= 0) & (diff <= window) & (diff % dilation == 0)
        mask = np.where(count > 0, np.log(np.maximum(count, 1)) / ATT_SCALE, NEG)
        const[:, col:col + diff.shape[1]] = mask
    const[:, C_FREQ:C_FREQ + 32] = np.float32(THETA) ** (-np.arange(0, HD, 2, dtype=np.float32) / np.float32(HD))
    return const


def kernel(**inputs):
    import concourse.bacc as bacc
    from concourse.bass_utils import run_bass_kernel_spmd

    nc = bacc.Bacc("TRN2", target_bir_lowering=False, num_devices=1, dynamic_dma_scratch_size=1024)
    arrays, aps = {}, {}

    def give(name, array):
        arrays[f"in_{name}"] = array
        aps[name] = nc.dram_tensor(f"in_{name}", array.shape, mybir.dt.from_np(array.dtype),
                                   kind="ExternalInput").ap()

    for name in _NAMES:
        array = np.ascontiguousarray(inputs[name])
        give(name, array.reshape(array.shape[1:]))
    give("final_norm", np.ascontiguousarray(inputs["final_norm"]))
    give("const", shape_constants())
    out = nc.dram_tensor("out", (S, D), F32, kind="ExternalOutput").ap()
    layer_program(nc, aps, out)
    r = run_bass_kernel_spmd(nc, [arrays], core_ids=[0])
    return r.results[0]["out"].reshape(1, S, D)
```

```python
from contextlib import ExitStack

import numpy as np

import concourse.bass as bass
from concourse import mybir

ALU = mybir.AluOpType
ACT = mybir.ActivationFunctionType
F32 = mybir.dt.float32
F32R = mybir.dt.float32r
I32 = mybir.dt.int32
AX_X = mybir.AxisListType.X

P = 128
D = 2048
S = 256
TT = S // P
FF = 5632
NC = 512
KT = D // P
AW = 1024
NH, HD = 16, 64
NG = 8
MH, MHD = 4, 512
EPS = 1e-6
THETA = 10000.0
ATT_SCALE = HD ** -0.5
MEM_SCALE = MHD ** -0.5
NEG = -1e30

RAW = 4
RING = 4
AHEAD = 4
FCH = FF // NC

FFN_HALVES = FCH * 24
M_F1 = 0
M_WIN = M_F1 + FFN_HALVES
M_MKV = M_WIN + 80
M_WO = M_MKV + 64
M_MQ = M_WO + 32
M_MO = M_MQ + 32
M_F2 = M_MO + 32
M_END = M_F2 + FFN_HALVES

U_F1 = 0
U_WIN = U_F1 + 2 * FCH
U_MKV = U_WIN + 5
U_WO = U_MKV + 4
U_MQ = U_WO + 2
U_MO = U_MQ + 2
U_F2 = U_MO + 2

G_FFN1, G_MIX, G_MEMQ, G_MEMKV, G_FFN2, G_ATTN, G_SGU, B_SGU = 0, 16, 32, 48, 64, 80, 88, 96
NVEC = 104

PAIRS = ("gv", "u", "q", "k", "v")
PAIR_COL = {"q": 0, "k": AW, "v": 2 * AW, "u": 3 * AW, "gv": 4 * AW}

C_ID, C_MASK, C_FREQ, C_END = 0, 128, 512, 544


def unit_numbers():
    order = [("gain1",)]
    order += [("x", j) for j in range(8)]
    order += [("a1", i, j) for i in range(FCH) for j in range(2)]
    order += [("cols",)] + [("h1", j) for j in range(8)] + [("ws", 0), ("ws", 1)]
    order += [("mem", j) for j in range(8)]
    for k in range(NH + 1):
        if k:
            order.append(("p", k - 1))
        if k < NH:
            if k % 2 == 0:
                order.append(("qk", k // 2))
            if k % 2 == 0 and 2 <= k <= 8:
                order += [("mk", k // 2 - 1, 0), ("mk", k // 2 - 1, 1)]
            if k % 2 and k < 8:
                order.append(("sgu", k // 2))
    order += [("att", j) for j in range(4)]
    order += [("h2", j) for j in range(8)]
    for c in range(MH):
        order += [("mq", c, 0), ("mq", c, 1), ("mp", c)]
    order += [("h3", j) for j in range(8)]
    order += [("a2", i, j) for i in range(FCH) for j in range(2)]
    number = {name: n for n, name in enumerate(order)}
    split = [n for n in order if n[0] in ("x", "a1", "h1", "mem", "sgu", "att", "h2", "h3", "a2")]
    return number, {name: n for n, name in enumerate(split)}


UNIT, SPLIT = unit_numbers()


def layer_program(nc, a, out):
    with ExitStack() as ctx:
        def sb(name, shape, dt=F32):
            return ctx.enter_context(nc.sbuf_tensor(name, shape, dt))

        def sem(name):
            return ctx.enter_context(nc.semaphore(name))

        h = sb("h", [P, TT, D])
        x_hi, x_lo = sb("x_hi", [P, KT, S], F32R), sb("x_lo", [P, KT, S], F32R)
        y_hi, y_lo = sb("y_hi", [P, KT, S], F32R), sb("y_lo", [P, KT, S], F32R)
        raw = sb("raw", [P, RAW, 4, NC])
        w_hi, w_lo = sb("w_hi", [P, RING, 2, NC], F32R), sb("w_lo", [P, RING, 2, NC], F32R)
        qk = sb("qk", [P, TT, 2, AW])
        v = sb("v", [P, TT, AW])
        memv = sb("memv", [P, TT, D])
        memk_t = sb("memk_t", [P, KT, S])
        att = sb("att", [P, TT, AW])
        tmp = sb("tmp", [P, 2048])
        junk = sb("junk", [P, NC])
        const = sb("const", [P, C_END])
        cols = sb("cols", [P, NVEC])
        trig = sb("trig", [P, 2, TT, 32])
        pos = sb("pos", [P, TT], I32)
        stat = sb("stat", [P, 72])

        ident = const[:, C_ID:C_ID + P]
        aT_hi, aT_lo = y_hi[:, 12:16, :], y_lo[:, 12:16, :]
        last_hi, last_lo = y_hi[:, 8:12, :], y_lo[:, 8:12, :]
        att_flat = att[:, :, :].rearrange("p t n -> p (t n)")
        silu = att_flat[:, 0:1024].rearrange("p (t n) -> p t n", t=TT)
        hid = att_flat[:, 1024:2048].rearrange("p (t n) -> p t n", t=TT)
        rope_tmp = att_flat[:, 0:1024].rearrange("p (r n) -> p r n", r=4)
        mem_nat = memk_t[:, :, :].rearrange("p k s -> p (k s)").rearrange("p (t n) -> p t n", t=TT)
        memv_flat = memv[:, :, :].rearrange("p t n -> p (t n)")
        u = memv_flat[:, 0:2048].rearrange("p (t n) -> p t n", t=TT)
        gv = memv_flat[:, 2048:4096].rearrange("p (t n) -> p t n", t=TT)
        mk_nat = memv_flat[:, 2048:3072].rearrange("p (t n) -> p t n", t=TT)
        ln_gain, ln_bias = tmp[:, 0:1024], tmp[:, 1024:2048]
        qk_t = tmp[:, 0:512]
        sm, pr, pr_t = tmp[:, 512:896], tmp[:, 896:1280], tmp[:, 1280:1664]
        qk_flat = qk[:, :, :, :].rearrange("p t w n -> p (t w n)")
        mq_nat = qk_flat[:, 0:1024].rearrange("p (t n) -> p t n", t=TT)
        mq_t = qk_flat[:, 1024:2048].rearrange("p (k s) -> p k s", k=4)
        mp = qk_flat[:, 2048:2560].rearrange("p (t m) -> p t m", t=TT)
        mp_t = qk_flat[:, 2560:3072].rearrange("p (m q) -> p m q", m=TT)
        ws_nat = qk_flat[:, 0:1024].rearrange("p (g j) -> p g j", g=NG)
        vec_rows = qk_flat[:, 1024:1152]
        v_flat = v[:, :, :].rearrange("p t n -> p (t n)")
        ws_t = att_flat[:, 1024:2048].rearrange("p (g i) -> p g i", g=NG)
        final_gain = v_flat
        y_out = mem_nat

        ssq = stat[:, 0:8].rearrange("p (t c) -> p t c", t=TT)
        var = stat[:, 8:10]
        rstd = stat[:, 10:12]
        n0, n1, n2 = stat[:, 12:14], stat[:, 14:16], stat[:, 16:18]
        mem_ssq = stat[:, 18:26].rearrange("p (t c) -> p t c", t=TT)
        mem_rstd = stat[:, 26:28]
        gv_sum = stat[:, 28:32].rearrange("p (t c) -> p t c", t=TT)
        gv_mean = stat[:, 32:34]
        gv_ssq = stat[:, 62:66].rearrange("p (t c) -> p t c", t=TT)
        gv_rstd = stat[:, 34:36]
        sgu_ssq = stat[:, 36:40].rearrange("p (t c) -> p t c", t=TT)
        sgu_rstd = stat[:, 40:42]
        att_ssq = stat[:, 42:50].rearrange("p (t c) -> p t c", t=TT)
        att_rstd = stat[:, 50:52]
        root = stat[:, 52:54]
        s_max, s_neg = stat[:, 54:56], stat[:, 56:58]
        s_sum, s_inv = stat[:, 58:60], stat[:, 60:62]

        bank = ctx.enter_context(nc.psum_tensor("bank", [P, 8, NC], F32))

        landed = [sem(f"slab_landed_{s}") for s in range(RAW)]
        hi_ready, lo_ready = sem("hi_ready"), sem("lo_ready")
        half_used = sem("half_used")
        pair_free = [sem(f"pair_free_{p}") for p in range(3)]
        tr_done = sem("tr_done")
        tr_hi = sem("tr_hi")
        tr_free = [sem("tr_free_6"), sem("tr_free_7")]
        squared, root_ready, var_ready = sem("squared"), sem("root_ready"), sem("var_ready")
        rstd_ready = sem("rstd_ready")
        const_in, vec_in, ws_in, ln_in, mem_in, pos_in = (
            sem(n) for n in ("const_in", "vec_in", "ws_in", "ln_in", "mem_in", "pos_in"))
        x_in = [sem(f"x_in_{c}") for c in range(4)]
        ident_in, gain1_in = sem("ident_in"), sem("gain1_in")
        x_first_in, w_first_in = sem("x_first_in"), sem("w_first_in")
        ws_masked = sem("ws_masked")
        trig_arg, trig_ready = sem("trig_arg"), sem("trig_ready")
        centred, gv_ready = sem("centred"), sem("gv_ready")
        sv_done, sgu_ready, sgu_scaled = sem("sv_done"), sem("sgu_ready"), sem("sgu_scaled")
        rope_done = sem("rope_done")
        s_done, s_masked, p_ready = sem("s_done"), sem("s_masked"), sem("p_ready")
        pv_done, o_ready, att_scaled = sem("pv_done"), sem("o_ready"), sem("att_scaled")
        ms_done, mmax_ready, mexp_ready = (sem(n) for n in ("ms_done", "mmax_ready", "mexp_ready"))
        mp_ready = sem("mp_ready")
        mo_hi = sem("mo_hi")
        mpv_done, mo_ready = sem("mpv_done"), sem("mo_ready")
        gain_in, out_done = sem("gain_in"), sem("out_done")
        y_left_ready, y_right_ready = sem("y_left_ready"), sem("y_right_ready")
        gained = sem("gained")
        tile_done = sem("tile_done")
        step = sem("vector_step")

        block = ctx.enter_context(nc.Block())

        def f32(ap):
            return ap.bitcast(F32)

        def pair_bank(pair, t):
            return bank[:, 2 * pair + t, :]

        def read_out(eng, pair, use, t=1):
            eng.wait_ge(pair_free[pair], 2 * use + t + 1)

        def ffn_final(uses, uses2):
            last = uses + 2 * FCH - 1
            return [(2, uses2 + 2 * FCH - 2), (0, last), (2, uses2 + 2 * FCH - 1), (1, last)]

        final = {"h1": ffn_final(U_F1, 0), "h2": [(c % 2, U_WO + c // 2) for c in range(4)],
                 "h3": [(c % 2, U_MO + c // 2) for c in range(4)], "h4": ffn_final(U_F2, 2 * FCH)}

        @block.sync
        def _(sp):
            def x_part(lo, hi, landed_x):
                sp.dma_start(h[:, :, lo:hi],
                             a["x"][:, lo:hi].rearrange("(t p) n -> p t n", p=P)).then_inc(landed_x, 16)

            def load(m, j, w, row, col):
                if not isinstance(m, int) or m >= 2 * RAW:
                    sp.wait_ge(lo_ready, m - 2 * RAW + 2)
                slot = (j // 2) % RAW
                src = w[bass.ds(row, 512), bass.ds(col, NC)].rearrange("(k p) n -> p k n", p=P)
                if isinstance(m, int) and m == 0:
                    sp.dma_start(raw[:, 0, 0:2, :], src[:, 0:2, :]).then_inc(w_first_in, 16)
                    x_part(2 * P, 4 * P, x_in[0])
                    sp.dma_start(raw[:, 0, 2:4, :], src[:, 2:4, :]).then_inc(landed[0], 16)
                    return
                sp.dma_start(raw[:, slot, :, :], src).then_inc(landed[slot], 16)

            def x_loads(s):
                if s == 0:
                    sp.dma_start(const[:, C_ID:C_ID + P], a["const"][:, C_ID:C_ID + P]).then_inc(ident_in, 16)
                    sp.dma_start(vec_rows[0:KT, :], a["ffn1_norm"].rearrange("(r c) -> r c", c=P))\
                        .then_inc(gain1_in, 16)
                    x_part(0, 2 * P, x_first_in)
                else:
                    x_part(s * NC, (s + 1) * NC, x_in[s])

            def other_loads(s):
                if s == 0:
                    sp.dma_start(const[:, C_MASK:C_END], a["const"][:, C_MASK:C_END]).then_inc(const_in, 16)
                    sp.dma_start(ws_nat, a["sgu_w_s"].rearrange("g i j -> i g j")).then_inc(ws_in, 16)
                    with nc.allow_non_contiguous_dma(reason="256 positions, one per partition and tile"):
                        sp.dma_start(pos[:, :], a["positions"].rearrange("(t p) -> p t", p=P)).then_inc(pos_in, 16)
                elif s == 1:
                    for at, name in ((G_MIX, "mix_norm"), (G_MEMQ, "mem_q_norm"), (G_MEMKV, "mem_kv_norm"),
                                     (G_FFN2, "ffn2_norm")):
                        sp.dma_start(vec_rows[at:at + KT, :], a[name].rearrange("(r c) -> r c", c=P))\
                            .then_inc(vec_in, 16)
                elif s == 2:
                    for at, name in ((G_ATTN, "attn_out_gain"), (G_SGU, "sgu_out_gain")):
                        sp.dma_start(vec_rows[at:at + NG, :], a[name].rearrange("(r c) -> r c", c=P))\
                            .then_inc(vec_in, 16)
                    sp.dma_start(vec_rows[B_SGU:B_SGU + NG, :], a["sgu_b_s"]).then_inc(vec_in, 16)
                else:
                    sp.dma_start(ln_gain, a["sgu_ln_gain"].partition_broadcast(P)).then_inc(ln_in, 16)
                    sp.dma_start(ln_bias, a["sgu_ln_bias"].partition_broadcast(P)).then_inc(ln_in, 16)
                    sp.dma_start(mem_nat, a["mem"].rearrange("(t p) n -> p t n", p=P)).then_inc(mem_in, 16)

            def ffn_loads(m0, gate, up, down, before=None, behind=None):
                for w, j0 in ((gate, 0), (up, 8)):
                    for s in range(4):
                        if before and j0 == 0:
                            before(s)
                        load(m0 + j0 + 2 * s, j0 + 2 * s, w, 512 * s, 0)
                        if behind and j0 == 8:
                            behind(s)
                with sp.Fori(0, FCH - 1) as i:
                    row, col, m = sp.snap(i * NC), sp.snap(i * NC + NC), sp.snap(i * 24 + (m0 + 16))
                    for w, j0 in ((gate, 0), (up, 8)):
                        for s in range(4):
                            load(m + (j0 + 2 * s), j0 + 2 * s, w, 512 * s, col)
                    for c in range(4):
                        load(m + (16 + 2 * c), 2 * c, down, row, NC * c)
                for c in range(4):
                    load(m0 + FFN_HALVES - 8 + 2 * c, 2 * c, down, (FCH - 1) * NC, NC * c)

            def square_loads(m0, w):
                with sp.Fori(0, D // NC) as c:
                    col, m = sp.snap(c * NC), sp.snap(c * 8 + m0)
                    for s in range(4):
                        load(m + 2 * s, 2 * s, w, 512 * s, col)

            ffn_loads(M_F1, a["ffn1_w_gate"], a["ffn1_w_up"], a["ffn1_w_down"], x_loads, other_loads)
            for n, name in enumerate(PAIRS):
                for c in range(2):
                    for s in range(4):
                        j = 16 * n + 8 * c + 2 * s
                        load(M_WIN + j, j, a["w_in"], 512 * s, PAIR_COL[name] + NC * c)
            square_loads(M_MKV, a["mem_w_k"])
            square_loads(M_MKV + 32, a["mem_w_v"])

            def mixed_loads(m0, w, row_a, row_b):
                order = [(c, r + 512 * s) for r in (row_a, row_b) for c in (0, 1) for s in range(2)]
                order += [(c, r + 512 * s) for c in (2, 3) for r in (row_a, row_b) for s in range(2)]
                for n, (c, row) in enumerate(order):
                    load(m0 + 2 * n, 2 * n, w, row, NC * c)

            mixed_loads(M_WO, a["w_out"], 1024, 0)
            square_loads(M_MQ, a["mem_w_q"])
            mixed_loads(M_MO, a["mem_w_o"], 0, 1024)
            ffn_loads(M_F2, a["ffn2_w_gate"], a["ffn2_w_up"], a["ffn2_w_down"])
            for t in range(TT):
                for c in range(2):
                    sp.wait_ge((y_left_ready, y_right_ready)[c], t + 1)
                    sp.dma_start(out[t * P:(t + 1) * P, c * AW:(c + 1) * AW],
                                 y_out[:, t, c * AW:(c + 1) * AW]).then_inc(out_done, 16)
            sp.wait_ge(out_done, 64)

        @block.gpsimd
        def _(pool):
            pool.wait_ge(ws_in, 16)
            nc.gpsimd.affine_select(out=ws_nat, in_=ws_nat, compare_op=ALU.is_ge, fill=0.0, base=0,
                                    pattern=[[0, NG], [-1, P]], channel_multiplier=1).then_inc(ws_masked, 1)

        @block.tensor
        def _(pe):
            def half(m, j, pair, kt, src_hi, src_lo, first, last):
                pe.wait_ge(lo_ready, m + 1)
                slot = j % RING
                for k in range(2):
                    for t in range(TT):
                        hi = src_hi[:, kt + k, t * P:(t + 1) * P]
                        lo = src_lo[:, kt + k, t * P:(t + 1) * P]
                        begin, end = first and k == 0, last and k == 1
                        o = pair_bank(pair, t)
                        nc.tensor.matmul(o, hi, w_hi[:, slot, k, :], start=begin, stop=False)
                        nc.tensor.matmul(o, hi, w_lo[:, slot, k, :], start=False, stop=False)
                        mm = nc.tensor.matmul(o, lo, w_hi[:, slot, k, :], start=False, stop=end)
                mm.then_inc(half_used, 1)

            def take_pair(pair, uses):
                if not isinstance(uses, int) or uses > 0:
                    pe.wait_ge(pair_free[pair], uses * 2)

            def unit_bank(n):
                if n >= 2:
                    pe.wait_ge(tr_free[n % 2], n // 2)
                return bank[:, 6 + n % 2, :]

            def transposed(n):
                pe.wait_ge(tr_free[n % 2], n // 2 + 1)

            def transpose_unit(n, src, kt):
                o = unit_bank(n)
                for k in range(2):
                    for t in range(TT):
                        tr = nc.tensor.transpose(o[:, (2 * k + t) * P:(2 * k + t + 1) * P],
                                                 src[:, t, (kt + k) * P:(kt + k + 1) * P], ident)
                tr.then_inc(tr_done, 1)

            def h_unit(name, j):
                read_out(pe, *final[name][j // 2])
                transpose_unit(UNIT[(name, j)], h, 2 * j)

            def square_chunk(m0, j0, pair, src_hi, src_lo, after, kts=(0, 2, 4, 6, 8, 10, 12, 14)):
                for j, kt in enumerate(kts):
                    half(m0 + j, j0 + j, pair, kt, src_hi, src_lo, j == 0, j == 7)
                    after(j)

            def nothing(j):
                pass

            def by_tiles(m, j, pair, src_hi, src_lo):
                pe.wait_ge(lo_ready, m + 2)
                for t in range(TT):
                    for k in range(4):
                        hi = src_hi[:, k, t * P:(t + 1) * P]
                        lo = src_lo[:, k, t * P:(t + 1) * P]
                        slot, o = (j + k // 2) % RING, pair_bank(pair, t)
                        nc.tensor.matmul(o, hi, w_hi[:, slot, k % 2, :], start=k == 0, stop=False)
                        nc.tensor.matmul(o, hi, w_lo[:, slot, k % 2, :], start=False, stop=False)
                        mm = nc.tensor.matmul(o, lo, w_hi[:, slot, k % 2, :], start=False, stop=k == 3)
                    mm.then_inc(tile_done, 1)

            def ffn(m0, uses, uses2, name, before_gate, after_down, last_chunk=None):
                def down(m, j0, u01, u2, a_hi, a_lo, after, last_chunk=None):
                    for c, (pair, used) in enumerate(((2, u2), (0, u01), (2, u2 + 1), (1, u01))):
                        take_pair(pair, used)
                        if c == 3 and last_chunk:
                            last_chunk(m + 2 * c, j0 + 2 * c, pair, a_hi, a_lo)
                            return
                        for n in range(2):
                            half(m + 2 * c + n, j0 + 2 * c + n, pair, 2 * n, a_hi, a_lo, n == 0, n == 1)
                        after(c)

                n0_ = UNIT[(name, 0, 0)]
                last = FCH - 1

                def turn(i, after):
                    m = i * 24 + (m0 + 16)
                    take_pair(0, i * 2 + (uses + 1))
                    square_chunk(m, 0, 0, x_hi, x_lo, nothing)
                    take_pair(1, i * 2 + (uses + 1))
                    for n in range(2):
                        b = (n0_ + n) % 2
                        pe.wait_ge(tr_free[b], i + (n0_ + n) // 2)
                        for k in range(2):
                            for t in range(TT):
                                tr = nc.tensor.transpose(
                                    bank[:, 6 + b, (2 * k + t) * P:(2 * k + t + 1) * P],
                                    hid[:, t, (2 * n + k) * P:(2 * n + k + 1) * P], ident)
                        tr.then_inc(tr_done, 1)
                    square_chunk(m + 8, 8, 1, x_hi, x_lo, nothing)
                    for n in range(2):
                        pe.wait_ge(tr_free[(n0_ + n) % 2], i + ((n0_ + n) // 2 + 1))
                    down(m + 16, 16, i * 2 + (uses + 2), i * 2 + uses2, aT_hi, aT_lo, after)

                take_pair(0, uses)
                for j in range(8):
                    before_gate(j)
                    half(m0 + j, j, 0, 2 * j, x_hi, x_lo, j == 0, j == 7)
                take_pair(1, uses)
                square_chunk(m0 + 8, 8, 1, x_hi, x_lo, nothing)
                with pe.Fori(0, last - 1) as i:
                    turn(i, nothing)

                def last_hidden(c):
                    if c == 1:
                        read_out(pe, 1, uses + 2 * FCH - 3)
                        for n in range(2):
                            transpose_unit(UNIT[(name, last, n)], hid, 2 * n)

                turn(last - 1, last_hidden)
                for n in range(2):
                    transposed(UNIT[(name, last, n)])
                down(m0 + FFN_HALVES - 8, 0, uses + 2 * FCH - 1, uses2 + 2 * FCH - 2, last_hi, last_lo, after_down,
                     last_chunk)

            pe.wait_ge(ident_in, 16)
            pe.wait_ge(gain1_in, 16)
            o = unit_bank(UNIT[("gain1",)])
            nc.tensor.transpose(o[:, 0:KT], vec_rows[0:KT, :], ident[0:KT, 0:KT]).then_inc(tr_done, 1)

            def ws_unit(n):
                pe.wait_ge(ws_masked, 1)
                o = unit_bank(UNIT[("ws", n)])
                for g in range(4):
                    tr = nc.tensor.transpose(o[:, g * P:(g + 1) * P], ws_nat[:, 4 * n + g, :], ident)
                tr.then_inc(tr_done, 1)

            def x_unit(j):
                if j < 2:
                    pe.wait_ge(x_in[0] if j else x_first_in, 16)
                elif j % 2 == 0:
                    pe.wait_ge(x_in[j // 2], 16)
                transpose_unit(UNIT[("x", j)], h, 2 * j)

            def x_units(j):
                if j == 0:
                    x_unit(0)
                if j + 1 < 8:
                    x_unit(j + 1)
                transposed(UNIT[("x", j)])

            def h1_units(c):
                if c == 0:
                    pe.wait_ge(vec_in, 7 * 16)
                    o = unit_bank(UNIT[("cols",)])
                    nc.tensor.transpose(o[:, 0:NVEC], vec_rows[0:NVEC, :], ident[0:NVEC, 0:NVEC]).then_inc(tr_done, 1)
                else:
                    h_unit("h1", 2 * c - 2)
                    h_unit("h1", 2 * c - 1)

            ffn(M_F1, U_F1, 0, "a1", x_units, h1_units)

            def last_h_units(name):
                transposed(UNIT[(name, 0)])

                def after(j):
                    if j in (1, 2):
                        h_unit(name, 5 + j)
                    if j in (3, 4) and name == "h1":
                        ws_unit(j - 3)
                    if j < 7:
                        transposed(UNIT[(name, j + 1)])
                return after

            take_pair(0, U_WIN)
            square_chunk(M_WIN, 0, 0, y_hi, y_lo, last_h_units("h1"))
            take_pair(1, U_WIN)
            square_chunk(M_WIN + 8, 8, 1, y_hi, y_lo, nothing)
            with pe.Fori(0, 3) as i:
                m = i * 16 + (M_WIN + 16)
                take_pair(0, i + (U_WIN + 1))
                square_chunk(m, 0, 0, y_hi, y_lo, nothing)
                take_pair(1, i + (U_WIN + 1))
                square_chunk(m + 8, 8, 1, y_hi, y_lo, nothing)

            def mem_units(j):
                if j == 0:
                    pe.wait_ge(mem_in, 16)
                transpose_unit(UNIT[("mem", j)], mem_nat, 2 * j)

            def spatial(j):
                if j % 2 or j > 6:
                    return
                t, n = j // 2 // 2, j // 2 % 2
                if j == 0:
                    transposed(UNIT[("ws", 1)])
                    pe.wait_ge(gv_ready, 2)
                    pe.wait_ge(pair_free[2], (2 * FCH) * 2)
                if t == 1:
                    pe.wait_ge(sgu_ready, 4 * n + 4)
                for g in range(4):
                    gg = 4 * n + g
                    mm = nc.tensor.matmul(bank[:, 4 + n, g * P:(g + 1) * P], ws_t[:, gg, :],
                                          gv[:, t, gg * P:(gg + 1) * P], start=True, stop=True)
                mm.then_inc(sv_done, 1)

            take_pair(0, U_WIN + 4)
            square_chunk(M_WIN + 64, 0, 0, y_hi, y_lo, mem_units)
            take_pair(1, U_WIN + 4)
            square_chunk(M_WIN + 72, 8, 1, y_hi, y_lo, spatial)

            def scores(k):
                if k % 2 == 0:
                    transposed(UNIT[("qk", k // 2)])
                if k:
                    pe.wait_ge(s_masked, k)
                else:
                    pe.wait_ge(sgu_ready, 16)
                r = HD * (k % 2)
                q, kk = qk_t[r:r + HD, 0:256], qk_t[r:r + HD, 256:512]
                nc.tensor.matmul(bank[:, 4, 0:P], q[:, 0:P], kk[:, 0:P], start=True, stop=True)
                nc.tensor.matmul(bank[:, 4, P:3 * P], q[:, P:2 * P], kk, start=True,
                                 stop=True).then_inc(s_done, 1)

            def p_unit(k):
                o = unit_bank(UNIT[("p", k)])
                pe.wait_ge(p_ready, k + 1)
                for b in range(3):
                    tr = nc.tensor.transpose(o[:, b * P:(b + 1) * P], pr[:, b * P:(b + 1) * P], ident)
                tr.then_inc(tr_done, 1)

            def weigh(k):
                transposed(UNIT[("p", k)])
                if k == 0:
                    read_out(pe, 0, U_WIN + 4)
                    read_out(pe, 1, U_WIN + 4)
                if k:
                    pe.wait_ge(o_ready, k)
                e = slice(HD * k, HD * k + HD)
                nc.tensor.matmul(bank[:, 5, 0:HD], pr_t[:, 0:P], v[:, 0, e], start=True, stop=True)
                nc.tensor.matmul(bank[:, 5, HD:2 * HD], pr_t[:, P:2 * P], v[:, 0, e], start=True, stop=False)
                nc.tensor.matmul(bank[:, 5, HD:2 * HD], pr_t[:, 2 * P:3 * P], v[:, 1, e], start=False,
                                 stop=True).then_inc(pv_done, 1)

            def qk_unit(g):
                o = unit_bank(UNIT[("qk", g)])
                for w in range(2):
                    for t in range(TT):
                        tr = nc.tensor.transpose(o[:, (2 * w + t) * P:(2 * w + t + 1) * P],
                                                 qk[:, t, w, g * P:(g + 1) * P], ident)
                tr.then_inc(tr_done, 1)

            pe.wait_ge(rope_done, 8)
            for j in range(8):
                transposed(UNIT[("mem", j)])
            for k in range(NH):
                pair, c, n = (k // 2) % 2, k // 2, k % 2
                if n == 0:
                    take_pair(pair, U_MKV + c // 2)
                m, j0 = M_MKV + 4 * k, 4 * n
                half(m, j0, pair, 8 * n, x_hi, x_lo, n == 0, False)
                if k:
                    p_unit(k - 1)
                if k % 2 == 0:
                    qk_unit(k // 2)
                half(m + 1, j0 + 1, pair, 8 * n + 2, x_hi, x_lo, False, False)
                if k:
                    weigh(k - 1)
                if k % 2 == 0 and 2 <= k <= 8:
                    read_out(pe, (k // 2 - 1) % 2, U_MKV + (k // 2 - 1) // 2)
                    transpose_unit(UNIT[("mk", k // 2 - 1, 0)], mk_nat, 0)
                half(m + 2, j0 + 2, pair, 8 * n + 4, x_hi, x_lo, False, False)
                scores(k)
                half(m + 3, j0 + 3, pair, 8 * n + 6, x_hi, x_lo, False, n == 1)
                if k % 2 == 0 and 2 <= k <= 8:
                    transpose_unit(UNIT[("mk", k // 2 - 1, 1)], mk_nat, 2)
                if k % 2 and k < 8:
                    if k == 1:
                        pe.wait_ge(sgu_scaled, 2)
                    transpose_unit(UNIT[("sgu", k // 2)], u, 2 * (k // 2))

            def mixed_phase(m0, uses, src_hi, src_lo, kt_a, kt_b, after, name):
                for n, (c, kt) in enumerate(((0, kt_a), (1, kt_a), (0, kt_b), (1, kt_b))):
                    if n < 2:
                        take_pair(c, uses)
                    for j in range(4):
                        half(m0 + 4 * n + j, 4 * n + j, c, kt + 2 * j, src_hi, src_lo,
                             n < 2 and j == 0, n >= 2 and j == 3)
                        after(4 * n + j)
                kts = tuple(range(kt_a, kt_a + 8, 2)) + tuple(range(kt_b, kt_b + 8, 2))

                def units(c):
                    def behind(j):
                        if c == 2 and j in (1, 2):
                            h_unit(name, j - 1)
                        if c == 2 and j in (4, 5):
                            h_unit(name, j - 2)
                        if c == 3 and j in (3, 4):
                            h_unit(name, j + 1)
                    return behind

                for c in (2, 3):
                    take_pair(c - 2, uses + 1)
                    square_chunk(m0 + 8 * c, 0, c - 2, src_hi, src_lo, units(c), kts)

            def last_head(j):
                if j == 0:
                    p_unit(NH - 1)
                if j == 1:
                    weigh(NH - 1)
                if j in (6, 7):
                    pe.wait_ge(att_scaled, 2)
                    for n in (2 * j - 12, 2 * j - 11):
                        transpose_unit(UNIT[("att", n)], att, 2 * n)
                if j in (7, 8, 9, 10):
                    transposed(UNIT[("att", j - 7)])

            for j in range(4):
                transposed(UNIT[("sgu", j)])
            mixed_phase(M_WO, U_WO, y_hi, y_lo, 8, 0, last_head, "h2")

            def memory_head(c, j):
                if j == 0:
                    read_out(pe, c % 2, U_MQ + c // 2)
                    for n in range(2):
                        transpose_unit(UNIT[("mq", c, n)], mq_nat, 2 * n)
                if j == 1:
                    for n in range(2):
                        transposed(UNIT[("mq", c, n)])
                    if c == 0:
                        for n in range(2):
                            transposed(UNIT[("mk", 3, n)])
                    else:
                        pe.wait_ge(mo_ready, 2 * c)
                    for t in range(TT):
                        for k in range(4):
                            mm = nc.tensor.matmul(bank[:, 4, t * S:(t + 1) * S], mq_t[:, k, t * P:(t + 1) * P],
                                                  memk_t[:, 4 * c + k, :], start=k == 0, stop=k == 3)
                    mm.then_inc(ms_done, 1)
                if j == 3:
                    o = unit_bank(UNIT[("mp", c)])
                    pe.wait_ge(mp_ready, 2 * c + 2)
                    for b in range(TT):
                        for t in range(TT):
                            tr = nc.tensor.transpose(o[:, (2 * b + t) * P:(2 * b + t + 1) * P],
                                                     mp[:, t, b * P:(b + 1) * P], ident)
                    tr.then_inc(tr_done, 1)
                if j == 4:
                    transposed(UNIT[("mp", c)])
                    if c == 0:
                        read_out(pe, 0, U_MKV + 3)
                        read_out(pe, 1, U_MKV + 3)
                    for n in range(2):
                        for k in range(2):
                            e = c * MHD + (2 * n + k) * P
                            for b in range(TT):
                                mm = nc.tensor.matmul(bank[:, 5 - n, k * S:(k + 1) * S], memv[:, b, e:e + P],
                                                      mp_t[:, b, :], start=b == 0, stop=b == 1)
                        mm.then_inc(mpv_done, 1)

            last_h2 = last_h_units("h2")
            for c in range(4):
                take_pair(c % 2, U_MQ + c // 2)
                square_chunk(M_MQ + 8 * c, 0, c % 2, x_hi, x_lo,
                             (lambda j, c=c: memory_head(c - 1, j)) if c else last_h2)

            def last_memory_head(j):
                memory_head(3, j)
                if j == 7:
                    pe.wait_ge(mo_ready, 8)

            pe.wait_ge(mo_ready, 6)
            mixed_phase(M_MO, U_MO, y_hi, y_lo, 0, 8, last_memory_head, "h3")

            last_h3 = last_h_units("h3")
            ffn(M_F2, U_F2, 2 * FCH, "a2", lambda j: last_h3(j - 1) if j else None, lambda c: None, by_tiles)

        @block.scalar
        def _(act):
            def split(m, j):
                if isinstance(m, int) and m >= M_END:
                    return
                slot, n = (j // 2) % RAW, j % 2
                if isinstance(m, int) and m == 0:
                    act.wait_ge(w_first_in, 16)
                elif n == 0 or (isinstance(m, int) and m == 1):
                    act.wait_ge(landed[slot], (m - j) * 2 + 16 * (j // 8 + 1))
                if not isinstance(m, int) or m >= RING:
                    act.wait_ge(half_used, m - RING + 1)
                nc.scalar.activation(w_hi[:, j % RING, :, :], raw[:, slot, 2 * n:2 * n + 2, :],
                                     ACT.Copy).then_inc(hi_ready, 1)

            def splits(m, j, count):
                for n in range(count):
                    split(m + (AHEAD + n), j + AHEAD + n)

            def read_unit_hi(n, dst_hi, kt, gain=None):
                act.wait_ge(tr_done, n + 1)
                src = bank[:, 6 + n % 2, :].rearrange("p (k s) -> p k s", k=2)
                if gain is None:
                    nc.scalar.activation(dst_hi[:, kt:kt + 2, :], src, ACT.Copy).then_inc(tr_hi, 1)
                else:
                    for k in range(2):
                        op = nc.scalar.activation(dst_hi[:, kt + k, :], src[:, k, :], ACT.Copy,
                                                  scale=cols[:, gain + k:gain + k + 1])
                    op.then_inc(tr_hi, 1)

            def read_unit(n, dst, width=NC):
                act.wait_ge(tr_done, n + 1)
                nc.scalar.activation(dst, bank[:, 6 + n % 2, 0:width], ACT.Copy).then_inc(tr_free[n % 2], 1)

            squares_done = [0]

            def squares(src, acc):
                if squares_done[0]:
                    act.wait_ge(squared, squares_done[0])
                squares_done[0] += 1
                nc.scalar.activation(junk[:, 0:src.shape[1]], src, ACT.Square,
                                     accum_out=acc).then_inc(squared, 1)

            def h_squares(name, c):
                for t in range(TT):
                    read_out(act, *final[name][c], t)
                    squares(h[:, t, c * NC:(c + 1) * NC], ssq[:, t, c:c + 1])

            roots = [0]

            def square_root(e=slice(0, TT)):
                roots[0] += 1
                act.wait_ge(var_ready, roots[0])
                nc.scalar.activation(root[:, e], var[:, e], ACT.Sqrt).then_inc(root_ready, 1)

            def ffn(m0, name, uses, before, last_units, h_name):
                n = before()
                splits(m0 + n, n, 8 - n)
                act.wait_ge(rstd_ready, {"a1": 1, "a2": 8}[name])
                act.wait_ge(half_used, m0 + 8)
                for t in range(TT):
                    nc.scalar.activation(silu[:, t, :], pair_bank(0, t), ACT.Silu,
                                         scale=rstd[:, t:t + 1]).then_inc(pair_free[0], 1)
                splits(m0 + 8, 8, 8)
                n0_ = UNIT[(name, 0, 0)]

                def turn(i, after):
                    m = i * 24 + (m0 + 16)
                    splits(m, 0, 8)
                    act.wait_ge(half_used, m + 8)
                    act.wait_ge(pair_free[1], i * 4 + (2 * uses + 2))
                    for t in range(TT):
                        nc.scalar.activation(silu[:, t, :], pair_bank(0, t), ACT.Silu,
                                             scale=rstd[:, t:t + 1]).then_inc(pair_free[0], 1)
                    for n in range(2):
                        act.wait_ge(tr_done, i * 2 + (n0_ + n + 1))
                        nc.scalar.activation(aT_hi[:, 2 * n:2 * n + 2, :],
                                             bank[:, 6 + (n0_ + n) % 2, :].rearrange("p (k s) -> p k s", k=2),
                                             ACT.Copy).then_inc(tr_hi, 1)
                    splits(m + 8, 8, 12)
                    after()
                    splits(m + 20, 20, 4)

                with act.Fori(0, FCH - 2) as i:
                    turn(i, lambda: None)

                def last_hidden():
                    for n in range(2):
                        read_unit_hi(UNIT[(name, FCH - 1, n)], last_hi, 2 * n)

                turn(FCH - 2, last_hidden)
                m = m0 + FFN_HALVES - 8
                for c in range(4):
                    splits(m + 2 * c, 2 * c, 2)
                    last_units(c)
                    if c:
                        h_squares(h_name, c - 1)

            def read_columns(name, count):
                n = UNIT[(name,)]
                act.wait_ge(tr_done, n + 1)
                nc.scalar.activation(cols[:, 0:count], bank[:, 6 + n % 2, 0:count], ACT.Copy)\
                    .then_inc(tr_free[n % 2], 1)
                act.wait_ge(tr_free[n % 2], n // 2 + 1)

            read_columns("gain1", KT)

            def first_splits():
                for j in range(8):
                    split(j, j)
                    read_unit_hi(UNIT[("x", j)], x_hi, 2 * j, G_FFN1 + 2 * j)
                act.wait_ge(x_first_in, 16)
                for c in range(4):
                    for t in range(TT):
                        act.wait_ge(x_in[c], 16)
                        squares(h[:, t, c * NC:(c + 1) * NC], ssq[:, t, c:c + 1])
                    splits(M_F1 + 4 + c, 4 + c, 1)
                square_root()
                return 8

            def h1_units(c):
                if c == 0:
                    read_columns("cols", NVEC)
                else:
                    for j in (2 * c - 2, 2 * c - 1):
                        read_unit_hi(UNIT[("h1", j)], y_hi, 2 * j, G_MIX + 2 * j)

            ffn(M_F1, "a1", U_F1, first_splits, h1_units, "h1")

            splits(M_WIN, 0, 2)
            for j in (6, 7):
                read_unit_hi(UNIT[("h1", j)], y_hi, 2 * j, G_MIX + 2 * j)
            splits(M_WIN + 2, 2, 1)
            h_squares("h1", 3)
            splits(M_WIN + 3, 3, 1)
            read_unit(UNIT[("ws", 0)], ws_t[:, 0:4, :].rearrange("p g i -> p (g i)"))
            splits(M_WIN + 4, 4, 1)
            read_unit(UNIT[("ws", 1)], ws_t[:, 4:8, :].rearrange("p g i -> p (g i)"))
            square_root()
            splits(M_WIN + 5, 5, 3)
            act.wait_ge(rstd_ready, 2)

            def tiles(dst, c):
                return [dst[:, t, c * NC:(c + 1) * NC] for t in range(TT)]

            m = M_WIN
            for c in range(2):
                if c:
                    splits(m + 8, 8, 8)
                act.wait_ge(half_used, m + 8 * c + 8)
                for t in range(TT):
                    nc.scalar.activation(tiles(gv, c)[t], pair_bank(c, t), ACT.Gelu_apprx_tanh,
                                         scale=rstd[:, t:t + 1], accum_out=gv_sum[:, t, c:c + 1])\
                        .then_inc(pair_free[c], 1)
            m = M_WIN + 16
            for c in range(2):
                splits(m + 8 * c, 8 * c, 6 - 3 * c)
                if c == 0:
                    for t in range(TT):
                        act.wait_ge(centred, t + 1)
                        for b in range(2):
                            squares(tiles(gv, b)[t], gv_ssq[:, t, b:b + 1])
                else:
                    square_root()
                    splits(m + 11, 11, 3)
                splits(m + 8 * c + 6, 8 * c + 6, 2)
                act.wait_ge(half_used, m + 8 * c + 8)
                for t in range(TT):
                    nc.scalar.activation(tiles(u, c)[t], pair_bank(c, t), ACT.Gelu_apprx_tanh,
                                         scale=rstd[:, t:t + 1]).then_inc(pair_free[c], 1)
            for w in range(2):
                m = M_WIN + 32 + 16 * w
                for c in range(2):
                    splits(m + 8 * c, 8 * c, 4)
                    if w == 1 and c == 0:
                        square_root()
                    splits(m + 8 * c + 4, 8 * c + 4, 4)
                    act.wait_ge(half_used, m + 8 * c + 8)
                    for t in range(TT):
                        nc.scalar.activation(qk[:, t, w, c * NC:(c + 1) * NC], pair_bank(c, t), ACT.Copy,
                                             scale=rstd[:, t:t + 1]).then_inc(pair_free[c], 1)
                    if w == 0 and c == 0:
                        act.wait_ge(trig_arg, 1)
                        nc.scalar.activation(trig[:, :, :, :], trig[:, :, :, :], ACT.Sin).then_inc(trig_ready, 1)
                    if w == 0 and c == 1:
                        act.wait_ge(mem_in, 16)
                        for t in range(TT):
                            for b in range(4):
                                squares(mem_nat[:, t, b * NC:(b + 1) * NC], mem_ssq[:, t, b:b + 1])
            m = M_WIN + 64
            for j in range(8):
                splits(m + j, j, 1)
                read_unit_hi(UNIT[("mem", j)], x_hi, 2 * j, G_MEMKV + 2 * j)
            for c in range(2):
                if c:
                    splits(m + 8, 8, 8)
                act.wait_ge(half_used, m + 8 * c + 8)
                for t in range(TT):
                    nc.scalar.activation(v[:, t, c * NC:(c + 1) * NC], pair_bank(c, t), ACT.Copy,
                                         scale=rstd[:, t:t + 1]).then_inc(pair_free[c], 1)

            def exponentials(k):
                act.wait_ge(s_masked, k + 1)
                if k:
                    act.wait_ge(tr_done, UNIT[("p", k - 1)] + 1)
                nc.scalar.activation(pr[:, 0:P], sm[:, 0:P], ACT.Exp, bias=s_neg[:, 0:1], scale=ATT_SCALE,
                                     accum_out=s_sum[:, 0:1])
                nc.scalar.activation(pr[:, P:3 * P], sm[:, P:3 * P], ACT.Exp, bias=s_neg[:, 1:2], scale=ATT_SCALE,
                                     accum_out=s_sum[:, 1:2]).then_inc(p_ready, 1)

            def att_squares(g):
                act.wait_ge(o_ready, 4 * g + 4)
                for t in range(TT):
                    squares(att[:, t, 256 * g:256 * g + 256], att_ssq[:, t, g:g + 1])

            act.wait_ge(rstd_ready, 4)
            for k in range(NH):
                m, n, c = M_MKV + 4 * k, k % 2, k // 2
                splits(m, 4 * n, 1)
                if k:
                    read_unit(UNIT[("p", k - 1)], pr_t, 3 * P)
                if k % 2 == 0:
                    read_unit(UNIT[("qk", k // 2)], qk_t)
                splits(m + 1, 4 * n + 1, 1)
                if k == 1:
                    square_root()
                if k % 2 == 0 and 2 <= k <= 8:
                    b = k // 2 - 1
                    read_unit(UNIT[("mk", b, 0)], memk_t[:, 4 * b:4 * b + 2, :].rearrange("p k s -> p (k s)"))
                splits(m + 2, 4 * n + 2, 1)
                exponentials(k)
                if k % 2 == 0 and 2 <= k <= 8:
                    read_unit(UNIT[("mk", b, 1)], memk_t[:, 4 * b + 2:4 * b + 4, :].rearrange("p k s -> p (k s)"))
                if k % 2 and k < 8:
                    read_unit_hi(UNIT[("sgu", k // 2)], y_hi, 8 + 2 * (k // 2), G_SGU + 2 * (k // 2))
                splits(m + 3, 4 * n + 3, 1)
                if k == 0:
                    act.wait_ge(sgu_ready, 16)
                    for t in range(TT):
                        for b in range(2):
                            squares(tiles(u, b)[t], sgu_ssq[:, t, b:b + 1])
                if n == 1:
                    act.wait_ge(half_used, m + 4)
                    for t in range(TT):
                        dst = mk_nat[:, t, :] if c < 4 else memv[:, t, (c - 4) * NC:(c - 3) * NC]
                        nc.scalar.activation(dst, pair_bank(c % 2, t), ACT.Copy,
                                             scale=mem_rstd[:, t:t + 1]).then_inc(pair_free[c % 2], 1)
                if k in (5, 9, 13):
                    att_squares(k // 4 - 1)

            def last_chunks(m, name, gain):
                splits(m, 0, 3)
                for c in range(2):
                    for j in (2 * c, 2 * c + 1):
                        read_unit_hi(UNIT[(name, j)], x_hi, 2 * j, gain + 2 * j)
                    h_squares(name, c)
                    splits(m + 3 + 3 * c, 3 + 3 * c, 3 - c)
                splits(m + 8, 0, 5)
                for j in (4, 5):
                    read_unit_hi(UNIT[(name, j)], x_hi, 2 * j, gain + 2 * j)
                h_squares(name, 2)
                splits(m + 13, 5, 3)

            m = M_WO
            splits(m, 0, 1)
            read_unit(UNIT[("p", NH - 1)], pr_t, 3 * P)
            splits(m + 1, 1, 1)
            att_squares(3)
            splits(m + 2, 2, 2)
            square_root()
            splits(m + 4, 4, 3)
            for j in range(4):
                if j == 2:
                    splits(m + 7, 7, 1)
                read_unit_hi(UNIT[("att", j)], y_hi, 2 * j, G_ATTN + 2 * j)
            splits(m + 8, 8, 8)
            last_chunks(m + 16, "h2", G_MEMQ)

            def memory_head(c, m, j0):
                splits(m, j0, 1)
                for n in range(2):
                    read_unit(UNIT[("mq", c, n)], mq_t[:, 2 * n:2 * n + 2, :].rearrange("p k s -> p (k s)"))
                splits(m + 1, j0 + 1, 1)
                act.wait_ge(mmax_ready, c + 1)
                for t in range(TT):
                    nc.scalar.activation(mp[:, t, :], bank[:, 4, t * S:(t + 1) * S], ACT.Exp, bias=s_neg[:, t:t + 1],
                                         scale=MEM_SCALE, accum_out=s_sum[:, t:t + 1]).then_inc(mexp_ready, 1)
                splits(m + 2, j0 + 2, 2)
                read_unit(UNIT[("mp", c)], mp_t.rearrange("p m q -> p (m q)"))
                splits(m + 4, j0 + 4, 1)
                for n in range(2):
                    act.wait_ge(mpv_done, 2 * c + n + 1)
                    nc.scalar.activation(y_hi[:, 4 * c + 2 * n:4 * c + 2 * n + 2, :],
                                         bank[:, 5 - n, :].rearrange("p (k s) -> p k s", k=2),
                                         ACT.Copy).then_inc(mo_hi, 1)
                splits(m + 5, j0 + 5, 3)

            for c in range(4):
                m = M_MQ + 8 * c
                if c == 0:
                    splits(m, 0, 2)
                    for j in (6, 7):
                        read_unit_hi(UNIT[("h2", j)], x_hi, 2 * j, G_MEMQ + 2 * j)
                    splits(m + 2, 2, 1)
                    h_squares("h2", 3)
                    splits(m + 3, 3, 2)
                    square_root()
                    splits(m + 5, 5, 3)
                    act.wait_ge(rstd_ready, 7)
                else:
                    memory_head(c - 1, m, 0)
                act.wait_ge(half_used, m + 8)
                for t in range(TT):
                    nc.scalar.activation(mq_nat[:, t, :], pair_bank(c % 2, t), ACT.Copy,
                                         scale=rstd[:, t:t + 1]).then_inc(pair_free[c % 2], 1)
            memory_head(3, M_MO, 0)
            splits(M_MO + 8, 8, 8)
            last_chunks(M_MO + 16, "h3", G_FFN2)

            def last_h3():
                splits(M_F2, 0, 2)
                for j in (6, 7):
                    read_unit_hi(UNIT[("h3", j)], x_hi, 2 * j, G_FFN2 + 2 * j)
                splits(M_F2 + 2, 2, 1)
                h_squares("h3", 3)
                splits(M_F2 + 3, 3, 2)
                square_root()
                return 5

            act.dma_start(final_gain, a["final_norm"].partition_broadcast(P)).then_inc(gain_in, 16)
            ffn(M_F2, "a2", U_F2, last_h3, lambda c: None, "h4")
            nc.scalar.activation(root, var, ACT.Sqrt)
            for t in range(TT):
                read_out(act, *final["h4"][3], t)
                squares(h[:, t, 3 * NC:D], ssq[:, t, 3:4])
                square_root(slice(t, t + 1))
                act.wait_ge(rstd_ready, 9 + t)
                act.wait_ge(gained, 4)
                nc.scalar.activation(y_out[:, t, 0:AW], y_out[:, t, 0:AW], ACT.Copy,
                                     scale=rstd[:, t:t + 1]).then_inc(y_left_ready, 1)

        @block.vector
        def _(dve):
            steps = [0]

            def link(ins):
                steps[0] += 1
                ins.then_inc(step, 1)
                dve.wait_ge(step, steps[0])

            def split(m, j):
                if isinstance(m, int) and m >= M_END:
                    return
                slot, n = (j // 2) % RAW, j % 2
                dve.wait_ge(hi_ready, m + 1)
                nc.vector.tensor_tensor(w_lo[:, j % RING, :, :], raw[:, slot, 2 * n:2 * n + 2, :],
                                        f32(w_hi[:, j % RING, :, :]), ALU.subtract).then_inc(lo_ready, 1)

            def splits(m, j, count):
                for n in range(count):
                    split(m + (AHEAD + n), j + AHEAD + n)

            def read_unit_lo(name, dst_hi, dst_lo, kt, gain=None):
                n = UNIT[name]
                dve.wait_ge(tr_hi, SPLIT[name] + 1)
                src = bank[:, 6 + n % 2, :].rearrange("p (k s) -> p k s", k=2)
                if gain is None:
                    nc.vector.tensor_tensor(dst_lo[:, kt:kt + 2, :], src, f32(dst_hi[:, kt:kt + 2, :]),
                                            ALU.subtract).then_inc(tr_free[n % 2], 1)
                else:
                    for k in range(2):
                        op = nc.vector.scalar_tensor_tensor(
                            dst_lo[:, kt + k, :], src[:, k, :], cols[:, gain + k:gain + k + 1],
                            f32(dst_hi[:, kt + k, :]), ALU.mult, ALU.subtract)
                    op.then_inc(tr_free[n % 2], 1)

            counts = {"squared": 0, "root": 0}

            def variance(acc, width, squares, e=slice(0, TT)):
                counts["squared"] += squares
                dve.wait_ge(squared, counts["squared"])
                link(nc.vector.tensor_reduce(n0[:, e], acc[:, e, :], AX_X, ALU.add))
                nc.vector.tensor_scalar(var[:, e], n0[:, e], 1.0 / width, EPS, ALU.mult, ALU.add).then_inc(var_ready, 1)

            def inverse_root(dst, e=slice(0, TT)):
                counts["root"] += 1
                dve.wait_ge(var_ready, counts["root"])
                dve.wait_ge(root_ready, counts["root"])
                n, r = n1[:, e], root[:, e]
                link(nc.vector.reciprocal(n, r))
                link(nc.vector.tensor_tensor(n, n, var[:, e], ALU.mult))
                link(nc.vector.tensor_tensor(n, n, r, ALU.add))
                link(nc.vector.tensor_scalar(n, n, 0.5, None, ALU.mult))
                nc.vector.reciprocal(dst[:, e], n).then_inc(rstd_ready, 1)
                dve.wait_ge(rstd_ready, counts["root"])

            def inverse_rms(acc, width, dst, parts):
                variance(acc, width, TT * parts)
                inverse_root(dst)

            def add_to_h(m_done, pair, c, scale):
                dve.wait_ge(half_used, m_done)
                for t in range(TT):
                    hc = h[:, t, c * NC:(c + 1) * NC]
                    op = nc.vector.scalar_tensor_tensor(hc, pair_bank(pair, t), scale, hc, ALU.mult, ALU.add)
                    op.then_inc(pair_free[pair], 1)

            def ffn(m0, name, before, last_units):
                def hidden(m_done):
                    dve.wait_ge(half_used, m_done)
                    for t in range(TT):
                        nc.vector.scalar_tensor_tensor(hid[:, t, :], pair_bank(1, t), rstd[:, t:t + 1],
                                                       silu[:, t, :], ALU.mult, ALU.mult).then_inc(pair_free[1], 1)

                n = before()
                splits(m0 + n, n, 16 - n)
                dve.wait_ge(pair_free[0], {"a1": 2, "a2": 2 * U_F2 + 2}[name])
                hidden(m0 + 16)
                base = {"a1": U_F1, "a2": U_F2}[name]
                base2 = {"a1": 0, "a2": 2 * FCH}[name]
                n0_, v0 = UNIT[(name, 0, 0)], SPLIT[(name, 0, 0)]

                def turn(i, after):
                    m = i * 24 + (m0 + 16)
                    splits(m, 0, 8)
                    for n in range(2):
                        dve.wait_ge(tr_hi, i * 2 + (v0 + n + 1))
                        nc.vector.tensor_tensor(
                            aT_lo[:, 2 * n:2 * n + 2, :],
                            bank[:, 6 + (n0_ + n) % 2, :].rearrange("p (k s) -> p k s", k=2),
                            f32(aT_hi[:, 2 * n:2 * n + 2, :]), ALU.subtract).then_inc(tr_free[(n0_ + n) % 2], 1)
                    splits(m + 8, 8, 8)
                    dve.wait_ge(pair_free[0], i * 4 + (2 * base + 4))
                    hidden(m + 16)
                    for c, pair in enumerate((2, 0, 2, 1)):
                        splits(m + 16 + 2 * c, 16 + 2 * c, 2)
                        dve.wait_ge(half_used, m + (16 + 2 * c + 2))
                        for t in range(TT):
                            hc = h[:, t, c * NC:(c + 1) * NC]
                            nc.vector.scalar_tensor_tensor(hc, pair_bank(pair, t), 0.5, hc, ALU.mult,
                                                           ALU.add).then_inc(pair_free[pair], 1)
                        if c == 1:
                            after()

                with dve.Fori(0, FCH - 2) as i:
                    turn(i, lambda: None)

                def last_hidden():
                    for n in range(2):
                        read_unit_lo((name, FCH - 1, n), last_hi, last_lo, 2 * n)

                turn(FCH - 2, last_hidden)
                m = m0 + FFN_HALVES - 8
                for c, pair in enumerate((2, 0, 2, 1)):
                    splits(m + 2 * c, 2 * c, 2)
                    if c == 3 and name == "a2":
                        return
                    add_to_h(m + 2 * c + 2, pair, c, 0.5)
                    last_units(c)

            def first_splits():
                for j in range(8):
                    split(j, j)
                    if j == 0:
                        dve.wait_ge(tr_free[0], 1)
                    read_unit_lo(("x", j), x_hi, x_lo, 2 * j, G_FFN1 + 2 * j)
                splits(M_F1 + 4, 4, 4)
                inverse_rms(ssq, D, rstd, 4)
                return 8

            def h1_units(c):
                if c == 0:
                    n = UNIT[("cols",)]
                    dve.wait_ge(tr_free[n % 2], n // 2 + 1)
                else:
                    for j in (2 * c - 2, 2 * c - 1):
                        read_unit_lo(("h1", j), y_hi, y_lo, 2 * j, G_MIX + 2 * j)

            ffn(M_F1, "a1", first_splits, h1_units)

            def angles():
                two_pi = 2 * np.pi
                magic = 1.5 * 2.0 ** 23

                def part(x, grid):
                    return float(np.round(x / grid) * grid)

                def parts(x):
                    p1 = part(x, 2.0 ** -10)
                    p2 = part(x - p1, 2.0 ** -22)
                    return p1, p2, float(np.float32(x - p1 - p2))

                c20 = parts(float(np.remainder(2.0 ** 20 + np.pi, two_pi) - np.pi))
                c10 = parts(float(np.remainder(2.0 ** 10 + np.pi, two_pi) - np.pi))
                cp = parts(two_pi)
                flat = [rope_tmp[:, r, 0:64] for r in range(4)]
                rest, n2, n1, n0_ = flat
                lowp = rope_tmp[:, 0, 64:128]
                posf = stat[:, 66:68]
                dve.wait_ge(pos_in, 16)
                dve.wait_ge(const_in, 16)
                link(nc.vector.tensor_copy(posf, pos[:, :]))
                for t in range(TT):
                    link(nc.vector.tensor_scalar(rest[:, 32 * t:32 * t + 32], const[:, C_FREQ:C_FREQ + 32],
                                                 posf[:, t:t + 1], None, ALU.mult))
                for dst, size in ((n2, 2.0 ** 20), (n1, 2.0 ** 10)):
                    link(nc.vector.tensor_scalar(dst, rest, 1 / size, magic, ALU.mult, ALU.add))
                    link(nc.vector.tensor_scalar(dst, dst, -magic, None, ALU.add))
                    link(nc.vector.scalar_tensor_tensor(rest, dst, -size, rest, ALU.mult, ALU.add))
                link(nc.vector.scalar_tensor_tensor(rest, n2, c20[0], rest, ALU.mult, ALU.add))
                link(nc.vector.scalar_tensor_tensor(rest, n1, c10[0], rest, ALU.mult, ALU.add))
                link(nc.vector.tensor_scalar(n0_, rest, 1 / two_pi, magic, ALU.mult, ALU.add))
                link(nc.vector.tensor_scalar(n0_, n0_, -magic, None, ALU.add))
                link(nc.vector.scalar_tensor_tensor(rest, n0_, -cp[0], rest, ALU.mult, ALU.add))
                link(nc.vector.tensor_scalar(lowp, n2, c20[1], None, ALU.mult))
                link(nc.vector.scalar_tensor_tensor(lowp, n1, c10[1], lowp, ALU.mult, ALU.add))
                link(nc.vector.scalar_tensor_tensor(lowp, n0_, -cp[1], lowp, ALU.mult, ALU.add))
                link(nc.vector.tensor_tensor(rest, rest, lowp, ALU.add))
                link(nc.vector.scalar_tensor_tensor(rest, n2, c20[2], rest, ALU.mult, ALU.add))
                link(nc.vector.scalar_tensor_tensor(rest, n1, c10[2], rest, ALU.mult, ALU.add))
                link(nc.vector.scalar_tensor_tensor(rest, n0_, -cp[2], rest, ALU.mult, ALU.add))
                link(nc.vector.tensor_scalar(n0_, rest, 1 / two_pi, magic, ALU.mult, ALU.add))
                link(nc.vector.tensor_scalar(n0_, n0_, -magic, None, ALU.add))
                link(nc.vector.scalar_tensor_tensor(rest, n0_, -float(np.float32(two_pi)), rest, ALU.mult, ALU.add))
                lim = float(np.nextafter(np.float32(np.pi), np.float32(0)))
                sin_arg = trig[:, 1, :, :].rearrange("p t f -> p (t f)")
                cos_arg = trig[:, 0, :, :].rearrange("p t f -> p (t f)")
                link(nc.vector.tensor_scalar(sin_arg, rest, lim, -lim, ALU.min, ALU.max))
                link(nc.vector.tensor_scalar(n0_, sin_arg, -1.0, None, ALU.mult))
                link(nc.vector.tensor_tensor(n0_, n0_, sin_arg, ALU.max))
                nc.vector.tensor_scalar(cos_arg, n0_, -1.0, float(np.pi / 2), ALU.mult, ALU.add)\
                    .then_inc(trig_arg, 1)

            splits(M_WIN, 0, 2)
            for j in (6, 7):
                read_unit_lo(("h1", j), y_hi, y_lo, 2 * j, G_MIX + 2 * j)
            splits(M_WIN + 2, 2, 3)
            inverse_rms(ssq, D, rstd, 4)
            splits(M_WIN + 5, 5, 11)

            m = M_WIN + 16
            splits(m, 0, 4)
            read_out(dve, 0, U_WIN)
            read_out(dve, 1, U_WIN)
            link(nc.vector.tensor_reduce(gv_mean, gv_sum, AX_X, ALU.add))
            link(nc.vector.tensor_scalar(gv_mean, gv_mean, 1.0 / AW, None, ALU.mult))
            for t in range(TT):
                nc.vector.tensor_scalar(gv[:, t, :], gv[:, t, :], gv_mean[:, t:t + 1], None,
                                        ALU.subtract).then_inc(centred, 1)
            splits(m + 4, 4, 4)
            variance(gv_ssq, AW, TT * 2)
            splits(m + 8, 8, 3)
            inverse_root(gv_rstd)
            dve.wait_ge(ln_in, 32)
            for t in range(TT):
                link(nc.vector.scalar_tensor_tensor(gv[:, t, :], gv[:, t, :], gv_rstd[:, t:t + 1], ln_gain,
                                                    ALU.mult, ALU.mult))
                nc.vector.tensor_tensor(gv[:, t, :], gv[:, t, :], ln_bias, ALU.add).then_inc(gv_ready, 1)
                splits(m + 11 + t, 11 + t, 1)
            splits(m + 13, 13, 3)

            def rotate(w, c):
                r4 = [rope_tmp[:, r, :].rearrange("p (e n) -> p e n", n=32) for r in range(4)]
                read_out(dve, c, U_WIN + 2 + w)
                for t in range(TT):
                    x4 = qk[:, t, w, c * NC:(c + 1) * NC].rearrange("p (e n) -> p e n", n=HD)
                    x1, x2 = x4[:, :, 0:32], x4[:, :, 32:64]
                    cos, sin = (trig[:, r, t, :].unsqueeze(1).to_broadcast([P, 8, 32]) for r in range(2))
                    nc.vector.tensor_tensor(r4[0], x1, cos, ALU.mult)
                    nc.vector.tensor_tensor(r4[1], x2, sin, ALU.mult)
                    nc.vector.tensor_tensor(r4[2], x1, sin, ALU.mult)
                    link(nc.vector.tensor_tensor(r4[3], x2, cos, ALU.mult))
                    nc.vector.tensor_tensor(x1, r4[0], r4[1], ALU.subtract)
                    nc.vector.tensor_tensor(x2, r4[2], r4[3], ALU.add).then_inc(rope_done, 1)
                    dve.wait_ge(rope_done, 4 * w + 2 * c + t + 1)

            m = M_WIN + 32
            splits(m, 0, 4)
            angles()
            splits(m + 4, 4, 8)
            dve.wait_ge(trig_ready, 1)
            rotate(0, 0)
            splits(m + 12, 12, 4)
            m = M_WIN + 48
            splits(m, 0, 4)
            rotate(0, 1)
            inverse_rms(mem_ssq, D, mem_rstd, 4)
            splits(m + 4, 4, 8)
            rotate(1, 0)
            splits(m + 12, 12, 4)
            m = M_WIN + 64
            for j in range(8):
                splits(m + j, j, 1)
                read_unit_lo(("mem", j), x_hi, x_lo, 2 * j, G_MEMKV + 2 * j)
                if j == 1:
                    rotate(1, 1)
            for j in range(8, 16):
                splits(m + j, j, 1)
                if j % 2 and 8 < j < 16:
                    b = (j - 9) // 2
                    t, n = b // 2, b % 2
                    dve.wait_ge(sv_done, b + 1)
                    read_out(dve, 1, U_WIN + 1)
                    for g in range(4):
                        gg = 4 * n + g
                        ug = u[:, t, gg * P:(gg + 1) * P]
                        nc.vector.scalar_tensor_tensor(ug, bank[:, 4 + n, g * P:(g + 1) * P],
                                                       cols[:, B_SGU + gg:B_SGU + gg + 1], ug, ALU.add,
                                                       ALU.mult).then_inc(sgu_ready, 1)

            def mask_scores(k):
                dve.wait_ge(s_done, k + 1)
                if k:
                    dve.wait_ge(p_ready, k)
                for t, (lo, hi) in enumerate(((0, P), (P, 3 * P))):
                    op = nc.vector.tensor_tensor_reduce(
                        out=sm[:, lo:hi], in0=bank[:, 4, lo:hi], in1=const[:, C_MASK + lo:C_MASK + hi],
                        scale=1.0, scalar=-3e38, op0=ALU.add, op1=ALU.max, accum_out=s_max[:, t:t + 1])
                link(op)
                nc.vector.tensor_scalar(s_neg, s_max, -ATT_SCALE, None, ALU.mult).then_inc(s_masked, 1)

            def head_out(k):
                link(nc.vector.reciprocal(s_inv, s_sum))
                dve.wait_ge(pv_done, k + 1)
                for t in range(TT):
                    op = nc.vector.tensor_scalar(att[:, t, HD * k:HD * k + HD], bank[:, 5, HD * t:HD * t + HD],
                                                 s_inv[:, t:t + 1], None, ALU.mult)
                op.then_inc(o_ready, 1)

            def scale_tiles(src, factor, done):
                for t in range(TT):
                    nc.vector.tensor_scalar(src[:, t, :], src[:, t, :], factor[:, t:t + 1], None,
                                            ALU.mult).then_inc(done, 1)

            for k in range(NH):
                m, n = M_MKV + 4 * k, k % 2
                splits(m, 4 * n, 2)
                if k:
                    head_out(k - 1)
                if k == 1:
                    inverse_rms(sgu_ssq, AW, sgu_rstd, 2)
                    scale_tiles(u, sgu_rstd, sgu_scaled)
                splits(m + 2, 4 * n + 2, 1)
                mask_scores(k)
                if k % 2 and k < 8:
                    read_unit_lo(("sgu", k // 2), y_hi, y_lo, 8 + 2 * (k // 2), G_SGU + 2 * (k // 2))
                splits(m + 3, 4 * n + 3, 1)

            def mixed_chunks(m, name, gain):
                splits(m + 8, 8, 4)
                add_to_h(m + 12, 0, 0, 1.0)
                splits(m + 12, 12, 4)
                add_to_h(m + 16, 1, 1, 1.0)
                m += 16
                splits(m, 0, 3)
                for c in range(2):
                    for j in (2 * c, 2 * c + 1):
                        read_unit_lo((name, j), x_hi, x_lo, 2 * j, gain + 2 * j)
                    splits(m + 3 + 3 * c, 3 + 3 * c, 3 - c)
                add_to_h(m + 8, 0, 2, 1.0)
                splits(m + 8, 0, 5)
                for j in (4, 5):
                    read_unit_lo((name, j), x_hi, x_lo, 2 * j, gain + 2 * j)
                splits(m + 13, 5, 3)
                add_to_h(m + 16, 1, 3, 1.0)

            m = M_WO
            splits(m, 0, 2)
            head_out(NH - 1)
            splits(m + 2, 2, 2)
            inverse_rms(att_ssq, AW, att_rstd, 4)
            scale_tiles(att, att_rstd, att_scaled)
            splits(m + 4, 4, 3)
            for j in range(4):
                if j == 2:
                    splits(m + 7, 7, 1)
                read_unit_lo(("att", j), y_hi, y_lo, 2 * j, G_ATTN + 2 * j)
            mixed_chunks(m, "h2", G_MEMQ)

            def memory_head(c, m, j0):
                splits(m, j0, 2)
                dve.wait_ge(ms_done, c + 1)
                link(nc.vector.tensor_reduce(s_max, bank[:, 4, :].rearrange("p (t m) -> p t m", t=TT), AX_X, ALU.max))
                nc.vector.tensor_scalar(s_neg, s_max, -MEM_SCALE, None, ALU.mult).then_inc(mmax_ready, 1)
                dve.wait_ge(mexp_ready, 2 * c + 2)
                link(nc.vector.reciprocal(s_inv, s_sum))
                for t in range(TT):
                    nc.vector.tensor_scalar(mp[:, t, :], mp[:, t, :], s_inv[:, t:t + 1], None,
                                            ALU.mult).then_inc(mp_ready, 1)
                splits(m + 2, j0 + 2, 3)
                for n in range(2):
                    dve.wait_ge(mo_hi, 2 * c + n + 1)
                    e = slice(4 * c + 2 * n, 4 * c + 2 * n + 2)
                    nc.vector.tensor_tensor(y_lo[:, e, :], bank[:, 5 - n, :].rearrange("p (k s) -> p k s", k=2),
                                            f32(y_hi[:, e, :]), ALU.subtract).then_inc(mo_ready, 1)
                splits(m + 5, j0 + 5, 3)

            for c in range(4):
                m = M_MQ + 8 * c
                if c == 0:
                    splits(m, 0, 2)
                    for j in (6, 7):
                        read_unit_lo(("h2", j), x_hi, x_lo, 2 * j, G_MEMQ + 2 * j)
                    splits(m + 2, 2, 3)
                    inverse_rms(ssq, D, rstd, 4)
                    splits(m + 5, 5, 3)
                else:
                    memory_head(c - 1, m, 0)
            memory_head(3, M_MO, 0)
            mixed_chunks(M_MO, "h3", G_FFN2)

            def last_h3():
                splits(M_F2, 0, 2)
                for j in (6, 7):
                    read_unit_lo(("h3", j), x_hi, x_lo, 2 * j, G_FFN2 + 2 * j)
                splits(M_F2 + 2, 2, 3)
                inverse_rms(ssq, D, rstd, 4)
                return 5

            def times_gain(c):
                if c == 0:
                    dve.wait_ge(gain_in, 16)
                read_out(dve, *final["h4"][c])
                for t in range(TT):
                    e = slice(c * NC, (c + 1) * NC)
                    nc.vector.tensor_tensor(y_out[:, t, e], h[:, t, e], final_gain[:, e],
                                            ALU.mult).then_inc(gained, 1)

            ffn(M_F2, "a2", last_h3, times_gain)

            def last_add(t):
                dve.wait_ge(tile_done, t + 1)
                hc = h[:, t, 3 * NC:D]
                nc.vector.scalar_tensor_tensor(hc, pair_bank(1, t), 0.5, hc, ALU.mult,
                                               ALU.add).then_inc(pair_free[1], 1)

            last_add(0)
            for t in range(TT):
                e = slice(t, t + 1)
                variance(ssq, D, (7, 1)[t], e)
                inverse_root(rstd, e)
                if t == 0:
                    last_add(1)
                dve.wait_ge(gained, 6)
                read_out(dve, *final["h4"][3], t)
                nc.vector.tensor_scalar(y_out[:, t, AW:3 * NC], y_out[:, t, AW:3 * NC], rstd[:, e], None, ALU.mult)
                nc.vector.scalar_tensor_tensor(y_out[:, t, 3 * NC:D], h[:, t, 3 * NC:D], rstd[:, e],
                                               final_gain[:, 3 * NC:D], ALU.mult, ALU.mult)\
                    .then_inc(y_right_ready, 1)


_NAMES = ("x", "mem", "positions", "ffn1_norm", "ffn1_w_gate", "ffn1_w_up", "ffn1_w_down", "mix_norm", "w_in",
          "sgu_ln_gain", "sgu_ln_bias", "sgu_w_s", "sgu_b_s", "attn_out_gain", "sgu_out_gain", "w_out",
          "mem_q_norm", "mem_kv_norm", "mem_w_q", "mem_w_k", "mem_w_v", "mem_w_o", "ffn2_norm",
          "ffn2_w_gate", "ffn2_w_up", "ffn2_w_down")


def shape_constants():
    const = np.zeros((P, C_END), np.float32)
    const[:, C_ID:C_ID + P] = np.eye(P, dtype=np.float32)
    i = np.arange(P)[:, None]
    for col, diff in ((C_MASK, i - np.arange(P)[None]), (C_MASK + P, i + P - np.arange(2 * P)[None])):
        count = np.zeros(diff.shape)
        for window, dilation in ((128, 1), (512, 4), (2048, 16)):
            count += (diff >= 0) & (diff <= window) & (diff % dilation == 0)
        mask = np.where(count > 0, np.log(np.maximum(count, 1)) / ATT_SCALE, NEG)
        const[:, col:col + diff.shape[1]] = mask
    const[:, C_FREQ:C_FREQ + 32] = np.float32(THETA) ** (-np.arange(0, HD, 2, dtype=np.float32) / np.float32(HD))
    return const


def kernel(**inputs):
    import concourse.bacc as bacc
    from concourse.bass_utils import run_bass_kernel_spmd

    nc = bacc.Bacc("TRN2", target_bir_lowering=False, num_devices=1, dynamic_dma_scratch_size=1024)
    arrays, aps = {}, {}

    def give(name, array):
        arrays[f"in_{name}"] = array
        aps[name] = nc.dram_tensor(f"in_{name}", array.shape, mybir.dt.from_np(array.dtype),
                                   kind="ExternalInput").ap()

    for name in _NAMES:
        array = np.ascontiguousarray(inputs[name])
        give(name, array.reshape(array.shape[1:]))
    give("final_norm", np.ascontiguousarray(inputs["final_norm"]))
    give("const", shape_constants())
    out = nc.dram_tensor("out", (S, D), F32, kind="ExternalOutput").ap()
    layer_program(nc, aps, out)
    r = run_bass_kernel_spmd(nc, [arrays], core_ids=[0])
    return r.results[0]["out"].reshape(1, S, D)
```
